# Optimizing a Trainium2 kernel written in Bass

```python
import jax, jax.numpy as jnp
from jax import lax
import numpy as np

D_MODEL = 1024
BATCH = 1
SEQ = 512
DEPTH = 1

N_META = 16
SB_BLOCK = 128
PAD = SB_BLOCK - N_META
SB_HEADS = 8
SB_HEAD_DIM = 64
SB_WIDTH = SB_HEADS * SB_HEAD_DIM
DN_HEADS = 8
DN_HEAD_DIM = 64
DN_WIDTH = DN_HEADS * DN_HEAD_DIM
DN_CONV = 4
DN_CHUNK = 64
PEER_HEADS = 8
PEER_N_KEYS = 128
PEER_N_EXPERTS = PEER_N_KEYS * PEER_N_KEYS
PEER_QUERY_DIM = 256
PEER_HALF = PEER_QUERY_DIM // 2
PEER_TOPK = 16
PEER_TOKEN_BLOCK = 256
EPS = 1e-6

IN_SPLITS = [SB_WIDTH, SB_WIDTH, SB_WIDTH, 3 * DN_WIDTH, DN_WIDTH, DN_HEADS, DN_HEADS, D_MODEL, D_MODEL]
IN_COLS = sum(IN_SPLITS)

kernel_name = "hybrid_stickbreak_gdn_peer_block"

def rms_norm(x, g):
    xf = x.astype(jnp.float32)
    y = xf * lax.rsqrt(jnp.mean(xf * xf, axis=-1, keepdims=True) + EPS)
    return (y * g.astype(jnp.float32)).astype(x.dtype)

def l2_norm(x):
    xf = x.astype(jnp.float32)
    return (xf * lax.rsqrt(jnp.sum(xf * xf, axis=-1, keepdims=True) + EPS)).astype(x.dtype)

def causal_depthwise_conv(x, w):
    K, C = w.shape
    return lax.conv_general_dilated(
        x, w[:, None, :].astype(x.dtype), window_strides=(1,), padding=[(K - 1, 0)],
        dimension_numbers=("NWC", "WIO", "NWC"), feature_group_count=C)

def stick_breaking_attention(q, k, v, key_valid):
    B, H, Lp, d = q.shape
    nb = Lp // SB_BLOCK
    scale = d ** -0.5
    qb = q.reshape(B, H, nb, SB_BLOCK, d).transpose(2, 0, 1, 3, 4)
    kpos = jnp.arange(Lp)

    def one_block(args):
        q_blk, i = args
        t = i * SB_BLOCK + jnp.arange(SB_BLOCK)
        z = jnp.einsum("bhqd,bhkd->bhqk", q_blk, k).astype(jnp.float32) * scale
        visible = (kpos[None, :] < t[:, None]) & key_valid[None, :]
        log_beta = jax.nn.log_sigmoid(z)
        log_one_minus = jnp.where(visible, jax.nn.log_sigmoid(-z), 0.0)
        log_remaining = lax.cumsum(log_one_minus, axis=3, reverse=True) - log_one_minus
        a = jnp.where(visible, jnp.exp(log_beta + log_remaining), 0.0)
        return jnp.einsum("bhqk,bhkd->bhqd", a.astype(v.dtype), v)

    out = lax.map(one_block, (qb, jnp.arange(nb)))
    return out.transpose(1, 2, 0, 3, 4).reshape(B, H, Lp, d)

def gated_delta_rule_chunked(q, k, v, beta, g):
    out_dtype = v.dtype
    f32 = jnp.float32
    B, H, Lp, dk = q.shape
    dv = v.shape[-1]
    C = DN_CHUNK
    n = Lp // C

    def chunk(a):
        return a.astype(f32).reshape(B, H, n, C, *a.shape[3:])

    q = chunk(q) * (dk ** -0.5)
    k, v, beta = chunk(k), chunk(v), chunk(beta)
    g = jnp.cumsum(chunk(g), axis=-1)
    idx = jnp.arange(C)
    lower_incl = idx[:, None] >= idx[None, :]
    strict_lower = idx[:, None] > idx[None, :]
    decay = jnp.exp(jnp.where(lower_incl, g[..., :, None] - g[..., None, :], -jnp.inf))
    k_beta = k * beta[..., None]
    v_beta = v * beta[..., None]
    m = jnp.where(strict_lower, jnp.einsum("bhncd,bhnsd->bhncs", k_beta, k) * decay, 0.0)
    eye = jnp.eye(C, dtype=f32)
    t_inv = lax.linalg.triangular_solve(eye + m, jnp.broadcast_to(eye, m.shape),
                                        left_side=True, lower=True, unit_diagonal=True)
    u = jnp.einsum("bhncs,bhnsd->bhncd", t_inv, v_beta)
    w = jnp.einsum("bhncs,bhnsd->bhncd", t_inv, k_beta * jnp.exp(g)[..., None])
    attn_intra = jnp.einsum("bhncd,bhnsd->bhncs", q, k) * decay
    q_decay = q * jnp.exp(g)[..., None]
    k_tail = k * jnp.exp(g[..., -1:] - g)[..., None]
    g_last = jnp.exp(g[..., -1])

    def step(S, inp):
        u_i, w_i, a_i, qd_i, kt_i, gl_i = inp
        v_new = u_i - jnp.einsum("bhcd,bhde->bhce", w_i, S)
        o = jnp.einsum("bhcd,bhde->bhce", qd_i, S) + jnp.einsum("bhcs,bhse->bhce", a_i, v_new)
        S = S * gl_i[..., None, None] + jnp.einsum("bhcd,bhce->bhde", kt_i, v_new)
        return S, o

    xs = (jnp.moveaxis(u, 2, 0), jnp.moveaxis(w, 2, 0), jnp.moveaxis(attn_intra, 2, 0),
          jnp.moveaxis(q_decay, 2, 0), jnp.moveaxis(k_tail, 2, 0), jnp.moveaxis(g_last, 2, 0))
    S0 = jnp.zeros((B, H, dk, dv), f32)
    _, o = lax.scan(step, S0, xs)
    return jnp.moveaxis(o, 0, 2).reshape(B, H, Lp, dv).astype(out_dtype)

def peer_ffn(h, w_q, sub_keys, u_tab, v_tab):
    B, L, D = h.shape
    T = B * L
    hf = h.reshape(T, D)
    q = (hf @ w_q).reshape(T, PEER_HEADS, 2, PEER_HALF)
    s = jnp.einsum("thpc,pkc->thpk", q, sub_keys.astype(q.dtype)).astype(jnp.float32)
    s1, i1 = lax.top_k(s[:, :, 0], PEER_TOPK)
    s2, i2 = lax.top_k(s[:, :, 1], PEER_TOPK)
    cand_s = (s1[..., :, None] + s2[..., None, :]).reshape(T, PEER_HEADS, PEER_TOPK * PEER_TOPK)
    cand_i = (i1[..., :, None] * PEER_N_KEYS + i2[..., None, :]).reshape(T, PEER_HEADS, PEER_TOPK * PEER_TOPK)
    top_s, pos = lax.top_k(cand_s, PEER_TOPK)
    expert_idx = jnp.take_along_axis(cand_i, pos, axis=-1)
    gate = jax.nn.softmax(top_s, axis=-1)

    HK = PEER_HEADS * PEER_TOPK
    nblk = -(-T // PEER_TOKEN_BLOCK)
    pad = nblk * PEER_TOKEN_BLOCK - T
    hp = jnp.pad(hf, ((0, pad), (0, 0))).reshape(nblk, PEER_TOKEN_BLOCK, D)
    ip = jnp.pad(expert_idx.reshape(T, HK), ((0, pad), (0, 0))).reshape(nblk, PEER_TOKEN_BLOCK, HK)
    gp = jnp.pad(gate.reshape(T, HK).astype(h.dtype), ((0, pad), (0, 0))).reshape(nblk, PEER_TOKEN_BLOCK, HK)

    def one_block(args):
        xb, ib, gb = args
        u = u_tab[ib]
        act = jax.nn.gelu(jnp.einsum("td,ted->te", xb, u), approximate=False)
        return jnp.einsum("te,ted->td", act * gb, v_tab[ib])

    y = lax.map(one_block, (hp, ip, gp)).reshape(nblk * PEER_TOKEN_BLOCK, D)[:T]
    return y.reshape(B, L, D)

def hybrid_layer(h, norm1_g, w_in, sb_q_norm_g, sb_k_norm_g, dn_conv_w, dn_a_log, dn_dt_bias,
                 dn_out_norm_g, w_sb_out, w_dn_out, w_o, norm2_g, peer_w_q, peer_sub_keys, peer_u, peer_v):
    B, L, D = h.shape
    f32 = jnp.float32
    xn = rms_norm(h, norm1_g)
    proj = xn @ w_in
    cuts = [int(c) for c in np.cumsum(IN_SPLITS)[:-1]]
    sb_q, sb_k, sb_v, dn_qkv, dn_z, dn_b, dn_a, gate_sb, gate_dn = jnp.split(proj, cuts, axis=-1)

    def heads(t, n_heads):
        return t.reshape(B, L, n_heads, -1).transpose(0, 2, 1, 3)

    def pad4(t):
        return jnp.pad(t, ((0, 0), (0, 0), (PAD, 0), (0, 0)))

    def pad3(t):
        return jnp.pad(t, ((0, 0), (0, 0), (PAD, 0)))

    q = rms_norm(heads(sb_q, SB_HEADS), sb_q_norm_g)
    k = rms_norm(heads(sb_k, SB_HEADS), sb_k_norm_g)
    v = heads(sb_v, SB_HEADS)
    key_valid = jnp.arange(L + PAD) >= PAD
    o_sb = stick_breaking_attention(pad4(q), pad4(k), pad4(v), key_valid)[:, :, PAD:]
    o_sb = o_sb.transpose(0, 2, 1, 3).reshape(B, L, SB_WIDTH)

    qkv = jax.nn.silu(causal_depthwise_conv(dn_qkv, dn_conv_w))
    dq, dk, dv = jnp.split(qkv, 3, axis=-1)
    dq = l2_norm(heads(dq, DN_HEADS))
    dk = l2_norm(heads(dk, DN_HEADS))
    dv = heads(dv, DN_HEADS)
    beta = jax.nn.sigmoid(dn_b.astype(f32)).transpose(0, 2, 1)
    g = (-jnp.exp(dn_a_log.astype(f32)) *
         jax.nn.softplus(dn_a.astype(f32) + dn_dt_bias.astype(f32))).transpose(0, 2, 1)
    o_dn = gated_delta_rule_chunked(pad4(dq), pad4(dk), pad4(dv), pad3(beta), pad3(g))[:, :, PAD:]
    o_dn = rms_norm(o_dn.transpose(0, 2, 1, 3), dn_out_norm_g) * jax.nn.silu(
        dn_z.reshape(B, L, DN_HEADS, DN_HEAD_DIM))
    o_dn = o_dn.reshape(B, L, DN_WIDTH)

    mix = jax.nn.sigmoid(gate_sb) * (o_sb @ w_sb_out) + jax.nn.sigmoid(gate_dn) * (o_dn @ w_dn_out)
    h = h + mix @ w_o

    h = h + peer_ffn(rms_norm(h, norm2_g), peer_w_q, peer_sub_keys, peer_u, peer_v)
    return h

def setup_inputs(seed: int = 0) -> dict:
    key = jax.random.key(seed)
    ks = jax.random.split(key, 20)
    f32 = jnp.float32

    def nrm(k, shape, s):
        return jax.random.normal(k, shape, f32) * s

    dt = jnp.exp(jax.random.uniform(ks[8], (DEPTH, DN_HEADS), f32, np.log(1e-3), np.log(1e-1)))
    return {
        "x": nrm(ks[0], (BATCH, SEQ, D_MODEL), 1.0),
        "meta_tokens": nrm(ks[1], (N_META, D_MODEL), 1.0),
        "norm1_g": 1.0 + nrm(ks[2], (DEPTH, D_MODEL), 0.02),
        "w_in": nrm(ks[3], (DEPTH, D_MODEL, IN_COLS), D_MODEL ** -0.5),
        "sb_q_norm_g": 1.0 + nrm(ks[4], (DEPTH, SB_HEAD_DIM), 0.02),
        "sb_k_norm_g": 1.0 + nrm(ks[5], (DEPTH, SB_HEAD_DIM), 0.02),
        "dn_conv_w": nrm(ks[6], (DEPTH, DN_CONV, 3 * DN_WIDTH), DN_CONV ** -0.5),
        "dn_a_log": jnp.log(jax.random.uniform(ks[7], (DEPTH, DN_HEADS), f32, 1.0, 16.0)),
        "dn_dt_bias": dt + jnp.log(-jnp.expm1(-dt)),
        "dn_out_norm_g": 1.0 + nrm(ks[9], (DEPTH, DN_HEAD_DIM), 0.02),
        "w_sb_out": nrm(ks[10], (DEPTH, SB_WIDTH, D_MODEL), SB_WIDTH ** -0.5),
        "w_dn_out": nrm(ks[11], (DEPTH, DN_WIDTH, D_MODEL), DN_WIDTH ** -0.5),
        "w_o": nrm(ks[12], (DEPTH, D_MODEL, D_MODEL), D_MODEL ** -0.5),
        "norm2_g": 1.0 + nrm(ks[13], (DEPTH, D_MODEL), 0.02),
        "peer_w_q": nrm(ks[14], (DEPTH, D_MODEL, PEER_HEADS * PEER_QUERY_DIM), D_MODEL ** -0.5),
        "peer_sub_keys": nrm(ks[15], (DEPTH, 2, PEER_N_KEYS, PEER_HALF), PEER_HALF ** -0.5),
        "peer_u": nrm(ks[16], (DEPTH, PEER_N_EXPERTS, D_MODEL), D_MODEL ** -0.5),
        "peer_v": nrm(ks[17], (DEPTH, PEER_N_EXPERTS, D_MODEL), 0.5),
    }

def reference(x, meta_tokens, norm1_g, w_in, sb_q_norm_g, sb_k_norm_g, dn_conv_w, dn_a_log, dn_dt_bias,
              dn_out_norm_g, w_sb_out, w_dn_out, w_o, norm2_g, peer_w_q, peer_sub_keys, peer_u, peer_v):
    B = x.shape[0]
    meta = jnp.broadcast_to(meta_tokens.astype(x.dtype)[None], (B, N_META, x.shape[-1]))
    h = jnp.concatenate([meta, x], axis=1)
    for l in range(DEPTH):
        h = hybrid_layer(h, norm1_g[l], w_in[l], sb_q_norm_g[l], sb_k_norm_g[l], dn_conv_w[l],
                         dn_a_log[l], dn_dt_bias[l], dn_out_norm_g[l], w_sb_out[l], w_dn_out[l], w_o[l],
                         norm2_g[l], peer_w_q[l], peer_sub_keys[l], peer_u[l], peer_v[l])
    return h[:, N_META:]


_drawn_inputs = setup_inputs


def setup_inputs(seed=0):
    import zlib

    import numpy as np

    out = dict(_drawn_inputs(seed))
    spreads = {}
    factors = {'sb_q_norm_g': 4.344, 'sb_k_norm_g': 4.16, 'dn_out_norm_g': 2.833}
    for name, (base, spread) in spreads.items():
        noise = np.random.default_rng([zlib.crc32(name.encode()), seed]).standard_normal(out[name].shape)
        drawn = base * np.exp(spread * noise) if base else spread * noise
        out[name] = __import__('jax').numpy.asarray(drawn.astype(out[name].dtype))
    for name, factor in factors.items():
        out[name] = (out[name] * factor).astype(out[name].dtype)
    return out
```

```python
from contextlib import ExitStack

import concourse.bass as bass
from concourse import mybir

ALU = mybir.AluOpType
ACT = mybir.ActivationFunctionType
F32 = mybir.dt.float32
F32R = mybir.dt.float32r
F16 = mybir.dt.float16
U32 = mybir.dt.uint32
AX_X = mybir.AxisListType.X

P = 128
D = 1024
DC = D // P
META = 16
SEQ = 512
TOK = META + SEQ
NT = SEQ // P
HEADS = 8
HD = 64
PAIRS = HEADS // 2
EPS = 1e-6
RING = 4
KEYS = 128
TOPK = 16
HK = HEADS * TOPK
LEVELS = 7


def tile_rows(n):
    return META if n == 0 else P


def tile_cols(n):
    return (0, META) if n == 0 else (META + (n - 1) * P, META + n * P)


def both(ap, count):
    p, w = ap.shape
    return ap.rearrange("p (a w) -> p a w", a=1).broadcast_to([p, count, w])


def wait_alone(eng, semaphore, value):
    with eng.register() as target:
        eng.reg_mov(target, value)
        eng.wait_ge(semaphore, 1)
        eng.wait_ge(semaphore, target)


class Turn:

    def __init__(self, eng, sem):
        self.eng, self.sem, self.base, self.count = eng, sem, 0, 0

    def __call__(self, instruction):
        self.count += 1
        instruction.then_inc(self.sem, 1)

    def wait(self):
        self.eng.wait_ge(self.sem, self.base + self.count)

    def then(self, instruction):
        self(instruction)
        self.wait()


class WeightStream:

    def __init__(self, sem, name):
        self.loaded = [sem(f"{name}_w_loaded{s}") for s in range(RING)]
        self.hi = sem(f"{name}_w_hi")
        self.lo = sem(f"{name}_w_lo")
        self.used = sem(f"{name}_w_used")
        self.evacuated = sem(f"{name}_evacuated")


def products(nc, out, stationary, moving, first, last):
    (sh, sl), (mh, ml) = stationary, moving
    nc.tensor.matmul(out, sh, mh, start=first, stop=False)
    nc.tensor.matmul(out, sh, ml, start=False, stop=False)
    return nc.tensor.matmul(out, sl, mh, start=False, stop=last)


def load_chunk(sp, st, ring, source, k, slot, turn, register):
    if register is not None or k >= RING:
        sp.wait_ge(st.lo, k - RING + 1)
    sp.dma_start(ring[:, slot, :, :], source).then_inc(st.loaded[slot], 16)


def build_constants(nc, ctx, c):
    sb = c["sb"]
    for name in ("ones", "negones", "ident", "tri", "neglow", "blocks"):
        c[name] = sb(ctx, name, [P, P])
    c["strict"] = sb(ctx, "strict", [P, P])
    c["levels"] = sb(ctx, "levels", [P, LEVELS, P])
    c["iota"] = sb(ctx, "iota", [P, P], F16)
    c["iotaf"] = sb(ctx, "iotaf", [P, TOPK])
    c["eps"] = sb(ctx, "eps", [P, 1])
    with ExitStack() as own:
        iota_int = sb(own, "iota_int", [P, P], mybir.dt.int32)
        turn_sem = own.enter_context(nc.semaphore("constant_steps"))
        iota_ready = own.enter_context(nc.semaphore("iota_ready"))
        block = own.enter_context(nc.Block())

        @block.gpsimd
        def _(pool):
            turn = Turn(pool, turn_sem)
            for name, value in (("ones", 1.0), ("negones", -1.0), ("ident", 0.0), ("tri", 1.0),
                                ("neglow", -1.0), ("blocks", 0.0), ("strict", 1.0)):
                turn(pool.memset(c[name][:, :], value))
            turn(pool.memset(c["levels"][:, :, :], 0.0))
            turn(pool.memset(c["eps"][:, :], EPS))
            pool.iota(iota_int[:, :], [[1, P]], base=0, channel_multiplier=0).then_inc(iota_ready, 1)
            pool.wait_ge(iota_ready, 1)
            turn.wait()
            turn.then(pool.memset(c["blocks"][0:HD, 0:HD], 1.0))
            turn.then(pool.memset(c["blocks"][HD:P, HD:P], 1.0))

            def select(ap, compare, fill, base, pattern, channel):
                turn(pool.affine_select(out=ap, in_=ap, compare_op=compare, fill=fill, base=base,
                                        pattern=pattern, channel_multiplier=channel))

            select(c["ident"][:, :], ALU.not_equal, 1.0, 0, [[-1, P]], 1)
            select(c["tri"][:, :], ALU.is_ge, 0.0, 0, [[1, P]], -1)
            select(c["strict"][:, :], ALU.is_gt, 0.0, 0, [[1, P]], -1)
            select(c["neglow"][:, :], ALU.is_ge, 0.0, 0, [[-1, P]], 1)
            for l in range(LEVELS):
                h = 1 << l
                nb = P // (2 * h)
                v = c["levels"][:, l, :].rearrange("p (b t w) -> p b t w", t=2, w=h)[:, :, 1, :]
                turn.wait()
                select(v, ALU.is_gt, 1.0, 0, [[2 * h, nb], [0, h]], -1)
                turn.wait()
                select(v, ALU.is_gt, 0.0, h, [[2 * h, nb], [0, h]], -1)
            turn.wait()

        @block.vector
        def _(dve):
            dve.wait_ge(iota_ready, 1)
            nc.vector.tensor_copy(c["iota"][:, :], iota_int[:, :])
            nc.vector.tensor_copy(c["iotaf"][:, :], iota_int[:, 0:TOPK])


def input_projections(nc, c, xT, w_v, w_full, w_xonly, w_ba, gains, gates_dram):
    with ExitStack() as own:
        sb = lambda name, shape, dt=F32: c["sb"](own, name, shape, dt)
        sem = lambda name: own.enter_context(nc.semaphore(name))
        x = sb("x", [P, DC, TOK])
        squares = sb("squares", [P, 2, TOK])
        rstd = squares[:, 0, :]
        xh = sb("xh", [P, DC, TOK], F32R)
        xl = sb("xl", [P, DC, TOK], F32R)
        ring = sb("w_ring", [P, RING, DC, P])
        ring_h = sb("ring_h", [P, RING, DC, P], F32R)
        ring_l = sb("ring_l", [P, RING, DC, P], F32R)
        ba_w = sb("ba_w", [P, DC, 16])
        ba_h = sb("ba_h", [P, DC, 16], F32R)
        ba_l = sb("ba_l", [P, DC, 16], F32R)
        gate_out = sb("gate_out", [P, 2, SEQ])
        ps = own.enter_context(nc.psum_tensor("psA", [P, 8, 512], F32))
        proj, qz, v, ba = c["proj"], c["qz"], c["v"], c["ba"]

        st = WeightStream(sem, "in")
        x_loaded = [sem(f"x_loaded{k}") for k in range(DC)]
        small_loaded = sem("small_loaded")
        squared, rooted = sem("squared"), sem("rooted")
        normed, x_hi, x_lo = sem("normed"), sem("x_hi"), sem("x_lo")
        ba_split, ba_hi_done = sem("ba_split"), sem("ba_hi_done")
        v_done, v_evacuated, ba_done = sem("v_done"), sem("v_evacuated"), sem("ba_done")
        gate_stored = [c["dma_sem"](f"gate_stored{s}") for s in range(2)]
        dve_steps, square_used = sem("dveA_steps"), sem("square_used")
        block = own.enter_context(nc.Block())
        n_full, n_qz, n_gate = 16, 8, 16
        k_full, k_qz = RING, RING + n_full
        k_gate = k_qz + n_qz

        @block.sync
        def _(sp):
            for k in range(DC):
                sp.dma_start(x[:, k, :], xT[k]).then_inc(x_loaded[k], 16)
                if k == 0:
                    sp.dma_start(c["gains"][:, :], gains).then_inc(small_loaded, 16)
                    sp.dma_start(ba_w[:, :, :], w_ba).then_inc(small_loaded, 16)
            for k in range(RING):
                sp.dma_start(ring[:, k, :, :], w_v[k]).then_inc(st.loaded[k], 16)
            for source, count, base, offset in ((w_full, n_full, k_full, 0), (w_xonly, n_qz + n_gate, k_qz, 0)):
                with sp.Fori(0, count // RING) as i:
                    for r in range(RING):
                        sp.wait_ge(st.lo, i * RING + (base + r - RING + 1))
                        sp.dma_start(ring[:, r, :, :], source[bass.ds(i * RING + r, 1)].rearrange(
                            "a p c f -> (a p) c f")).then_inc(st.loaded[r], 16)

        @block.scalar
        def _(act):
            for k in range(DC):
                act.wait_ge(x_loaded[k], 16)
                if k >= 2:
                    act.wait_ge(square_used, k - 1)
                nc.scalar.activation(squares[:, k % 2, :], x[:, k, :], ACT.Square).then_inc(squared, 1)
            act.wait_ge(square_used, DC)
            nc.scalar.activation(rstd[:, META:TOK], ps[:, 5, :], ACT.Sqrt, bias=c["eps"][:, :], scale=1.0 / D)
            nc.scalar.activation(rstd[:, 0:META], ps[:, 6, 0:META], ACT.Sqrt, bias=c["eps"][:, :],
                                 scale=1.0 / D).then_inc(rooted, 1)
            act.wait_ge(small_loaded, 32)
            nc.scalar.activation(ba_h[:, :, :], ba_w[:, :, :], ACT.Copy).then_inc(ba_hi_done, 1)
            for k in range(DC):
                act.wait_ge(normed, k + 1)
                nc.scalar.activation(xh[:, k, :], x[:, k, :], ACT.Copy).then_inc(x_hi, 1)

            def hi(slot, loads, used):
                act.wait_ge(st.loaded[slot], loads)
                if used is not None:
                    act.wait_ge(st.used, used)
                nc.scalar.activation(ring_h[:, slot, :, :], ring[:, slot, :, :], ACT.Copy).then_inc(st.hi, 1)

            for k in range(RING):
                hi(k, 16, None)
            act.wait_ge(v_done, NT + 1)
            with act.Fori(0, (n_full + n_qz) // RING) as i:
                for r in range(RING):
                    hi(r, i * 16 + 32, i * RING + (r + 1))
            with act.Fori(0, n_gate // RING) as i:
                for r in range(RING):
                    hi(r, i * 16 + 16 * (k_gate // RING) + 16, i * RING + (k_gate - RING + r + 1))

        @block.gpsimd
        def _(pool):
            with pool.Fori(0, n_gate // RING) as i:
                for r in range(RING):
                    pool.wait_ge(st.evacuated, i * RING + (k_gate + r + 1))
                    pool.dma_start(gates_dram[bass.ds(i * RING + r, 1)].rearrange("a p t -> (a p) t"),
                                   gate_out[:, r % 2, :]).then_inc(gate_stored[r % 2], 16)
            for r in range(2):
                pool.wait_ge(gate_stored[r], 16 * (n_gate // 2))

        @block.vector
        def _(dve):
            turn = Turn(dve, dve_steps)
            dve.wait_ge(rooted, 1)
            turn.then(nc.vector.reciprocal(rstd, rstd))
            dve.wait_ge(small_loaded, 32)
            for k in range(DC):
                nc.vector.scalar_tensor_tensor(out=x[:, k, :], in0=x[:, k, :], scalar=c["gains"][:, k:k + 1],
                                               in1=rstd, op0=ALU.mult, op1=ALU.mult).then_inc(normed, 1)
            dve.wait_ge(ba_hi_done, 1)
            nc.vector.tensor_tensor(ba_l[:, :, :], ba_w[:, :, :], ba_h[:, :, :].bitcast(F32),
                                    ALU.subtract).then_inc(ba_split, 1)
            for k in range(DC):
                dve.wait_ge(x_hi, k + 1)
                nc.vector.tensor_tensor(xl[:, k, :], x[:, k, :], xh[:, k, :].bitcast(F32),
                                        ALU.subtract).then_inc(x_lo, 1)

            def lo(slot, his):
                dve.wait_ge(st.hi, his)
                nc.vector.tensor_tensor(ring_l[:, slot, :, :], ring[:, slot, :, :],
                                        ring_h[:, slot, :, :].bitcast(F32), ALU.subtract).then_inc(st.lo, 1)

            for k in range(RING):
                lo(k, k + 1)
            for n in range(NT + 1):
                dve.wait_ge(v_done, n + 1)
                nc.vector.tensor_copy(v[0:tile_rows(n), n, :], ps[0:tile_rows(n), n % 2, :]).then_inc(v_evacuated, 1)
            lo(0, RING + 1)
            lo(1, RING + 2)
            dve.wait_ge(ba_done, 1)
            nc.vector.tensor_copy(ba[:, :, :], ps[:, 4, 0:(NT + 1) * 16].rearrange("p (n s) -> p n s", s=16)
                                  ).then_inc(st.evacuated, RING)
            with dve.Fori(0, n_full // RING) as i:
                for r in range(RING):
                    lo((r + 2) % RING, i * RING + (k_full + r + 3))
                    dve.wait_ge(st.used, i * RING + (k_full + r + 1))
                    dst = proj[:, bass.ds(i * RING + r, 1), :].rearrange("p a t -> p (a t)")
                    nc.vector.tensor_copy(dst[:, META:TOK], ps[:, 2 + r % 2, :])
                    nc.vector.tensor_copy(dst[:, 0:META], ps[:, 6 + r % 2, 0:META]).then_inc(st.evacuated, 1)
            with dve.Fori(0, n_qz // RING) as i:
                for r in range(RING):
                    lo((r + 2) % RING, i * RING + (k_qz + r + 3))
                    dve.wait_ge(st.used, i * RING + (k_qz + r + 1))
                    nc.vector.tensor_copy(qz[:, bass.ds(i * RING + r, 1), :].rearrange("p a t -> p (a t)"),
                                          ps[:, 2 + r % 2, :]).then_inc(st.evacuated, 1)

            def gate_chunk(r, at, stored, last=False):
                if not (last and r >= RING - 2):
                    lo((r + 2) % RING, at + 3)
                dve.wait_ge(st.used, at + 1)
                if stored is not None:
                    dve.wait_ge(gate_stored[r % 2], stored)
                nc.vector.tensor_copy(gate_out[:, r % 2, :], ps[:, 2 + r % 2, :]).then_inc(st.evacuated, 1)

            for r in range(RING):
                gate_chunk(r, k_gate + r, 16 if r >= 2 else None)
            with dve.Fori(1, n_gate // RING - 1) as i:
                for r in range(RING):
                    gate_chunk(r, i * RING + (k_gate + r), i * 32 + 16 * (r // 2))
            i = n_gate // RING - 1
            for r in range(RING):
                gate_chunk(r, i * RING + (k_gate + r), i * 32 + 16 * (r // 2), last=True)

        @block.tensor
        def _(pe):
            for k in range(DC):
                pe.wait_ge(squared, k + 1)
                nc.tensor.matmul(ps[:, 5, :], c["ones"][:, :], squares[:, k % 2, META:TOK], start=k == 0,
                                 stop=k == DC - 1)
                nc.tensor.matmul(ps[:, 6, 0:META], c["ones"][:, :], squares[:, k % 2, 0:META], start=k == 0,
                                 stop=k == DC - 1).then_inc(square_used, 1)
            pe.wait_ge(x_lo, DC)
            pe.wait_ge(st.lo, RING)

            def stationary_tokens(n, k):
                lo_col = 0 if n == 0 else tile_cols(n)[0]
                return tuple(part[:, k, lo_col:lo_col + P] for part in (xh, xl))

            for n in range(NT + 1):
                if n >= 2:
                    pe.wait_ge(v_evacuated, n - 1)
                for k in range(DC):
                    last = products(nc, ps[:, n % 2, :].rearrange("p (s f) -> p s f", s=RING),
                                    stationary_tokens(n, k), (ring_h[:, :, k, :], ring_l[:, :, k, :]),
                                    k == 0, k == DC - 1)
                last.then_inc(v_done, 1)
            nc.tensor.nop().then_inc(st.used, RING)
            pe.wait_ge(ba_split, 1)
            for n in range(NT + 1):
                for k in range(DC):
                    last = products(nc, ps[:, 4, n * 16:(n + 1) * 16], stationary_tokens(n, k),
                                    (ba_h[:, k, :], ba_l[:, k, :]), k == 0, k == DC - 1)
            last.then_inc(ba_done, 1)

            def chunk(r, at, meta):
                pe.wait_ge(st.lo, at + 1)
                pe.wait_ge(st.evacuated, at - 1)
                for k in range(DC):
                    w = (ring_h[:, r, k, :], ring_l[:, r, k, :])
                    last = products(nc, ps[:, 2 + r % 2, :], w, (xh[:, k, META:TOK], xl[:, k, META:TOK]),
                                    k == 0, k == DC - 1)
                    if meta:
                        last = products(nc, ps[:, 6 + r % 2, 0:META], w, (xh[:, k, 0:META], xl[:, k, 0:META]),
                                        k == 0, k == DC - 1)
                last.then_inc(st.used, 1)

            with pe.Fori(0, n_full // RING) as i:
                for r in range(RING):
                    chunk(r, i * RING + (k_full + r), True)
            with pe.Fori(0, (n_qz + n_gate) // RING) as i:
                for r in range(RING):
                    chunk(r, i * RING + (k_qz + r), False)


def token_scalars(nc, c):
    with ExitStack() as own:
        sb = lambda name, shape: c["sb"](own, name, shape, F32)
        sem = lambda name: own.enter_context(nc.semaphore(name))
        shape = [P, NT + 1, HEADS]
        y, soft, decay = sb("dt_shifted", shape), sb("dt_soft", shape), sb("decay_rate", [P, HEADS])
        exp_g = sb("exp_g", shape)
        ps = own.enter_context(nc.psum_tensor("psT", [P, 2, 512], F32))
        g, beta, G, neg_beta_exp, tail, last = (c["scalars"][:, k, :, :] for k in range(6))
        beta_done, rate_done, shifted = sem("beta_done"), sem("rate_done"), sem("shifted")
        soft_done, g_done, G_done = sem("soft_done"), sem("g_done"), sem("G_done")
        tail_args, exps_done = sem("tail_args"), sem("exps_done")
        act_steps, dve_steps = sem("actT_steps"), sem("dveT_steps")
        block = own.enter_context(nc.Block())
        a_log, dt_bias = c["small"][:, 0:8], c["small"][:, 8:16]

        @block.scalar
        def _(act):
            turn = Turn(act, act_steps)
            nc.scalar.activation(beta, c["ba"][:, :, 0:8], ACT.Sigmoid).then_inc(beta_done, 1)
            nc.scalar.activation(decay[:, :], a_log, ACT.Exp).then_inc(rate_done, 1)
            act.wait_ge(shifted, 1)
            turn.then(nc.scalar.activation(soft[:, :, :], soft[:, :, :], ACT.Exp, scale=-1.0))
            nc.scalar.activation(soft[:, :, :], soft[:, :, :], ACT.Ln, bias=c["ones"][:, 0:1]).then_inc(soft_done, 1)
            act.wait_ge(tail_args, 1)
            nc.scalar.activation(exp_g[:, :, :], G, ACT.Exp)
            nc.scalar.activation(tail, tail, ACT.Exp)
            nc.scalar.activation(last, last, ACT.Exp).then_inc(exps_done, 1)

        @block.vector
        def _(dve):
            turn = Turn(dve, dve_steps)
            shift = dt_bias.rearrange("p (a h) -> p a h", a=1).broadcast_to(shape)
            turn.then(nc.vector.tensor_tensor(y[:, :, :], c["ba"][:, :, 8:16], shift, ALU.add))
            nc.vector.scalar_tensor_tensor(out=soft[:, :, :], in0=y[:, :, :], scalar=-1.0, in1=y[:, :, :],
                                           op0=ALU.mult, op1=ALU.max).then_inc(shifted, 1)
            dve.wait_ge(soft_done, 1)
            turn.then(nc.vector.scalar_tensor_tensor(out=soft[:, :, :], in0=y[:, :, :], scalar=0.0, in1=soft[:, :, :],
                                                     op0=ALU.max, op1=ALU.add))
            dve.wait_ge(rate_done, 1)
            rate = decay[:, :].rearrange("p (a h) -> p a h", a=1).broadcast_to(shape)
            nc.vector.scalar_tensor_tensor(out=g, in0=soft[:, :, :], scalar=-1.0, in1=rate, op0=ALU.mult,
                                           op1=ALU.mult).then_inc(g_done, 1)
            dve.wait_ge(G_done, 1)
            sums = ps[:, 0, 0:40].rearrange("p (n h) -> p n h", h=HEADS)
            totals = ps[:, 1, 0:40].rearrange("p (n h) -> p n h", h=HEADS)
            turn(nc.vector.tensor_copy(G, sums))
            turn.then(nc.vector.tensor_copy(last, totals))
            turn.then(nc.vector.tensor_tensor(tail, last, G, ALU.subtract))
            nc.vector.tensor_scalar(tail, tail, 0.0, None, ALU.min).then_inc(tail_args, 1)
            dve.wait_ge(exps_done, 1)
            dve.wait_ge(beta_done, 1)
            nc.vector.scalar_tensor_tensor(out=neg_beta_exp, in0=exp_g[:, :, :], scalar=-1.0, in1=beta, op0=ALU.mult,
                                           op1=ALU.mult)

        @block.tensor
        def _(pe):
            pe.wait_ge(g_done, 1)
            nc.tensor.matmul(ps[:, 0, 0:40], c["tri"][:, :], g, start=True, stop=True)
            nc.tensor.matmul(ps[:, 1, 0:8], c["ones"][0:META, :], c["scalars"][0:META, 0, 0, :], start=True, stop=True)
            nc.tensor.matmul(ps[:, 1, 8:40], c["ones"][:, :], c["scalars"][:, 0, 1:, :], start=True,
                             stop=True).then_inc(G_done, 1)


ATT = [(e, kb) for e in range(2) for kb in range(NT, -1, -1)]
DIAG = [x for x in ATT if x[1] > 0]
LEVEL_TILES = [(l, n) for l in range(LEVELS) for n in range(NT + 1) if n > 0 or l < 4]
STEP_TILES = [x for x in LEVEL_TILES if x[0] > 0]
UNITS = [("z", 0), ("z", 1), ("soft", 0)]
for _a in range(len(ATT)):
    UNITS += [("products" if _a % 2 else "level", _a // 2 + 1), ("cum", _a)]
    UNITS += [("z", _a + 2)] if _a + 2 < len(ATT) else []
    UNITS += [("soft", _a + 1)] if _a + 1 < len(ATT) else []
UNITS += [("level", 6), ("pv", 0), ("pv", 1), ("products", 6)]
A_OFF = {4: 0, 3: 128, 2: 384, 1: 768, 0: 1280}
A_COLS = 1792


def first_query(kb):
    return max(kb - 1, 0) * P


def head_pairs(nc, c):
    with ExitStack() as own:
        sb = lambda name, shape, dt=F32: c["sb"](own, name, shape, dt)
        sem = lambda name: own.enter_context(nc.semaphore(name))
        norm_work = sb("norm_work", [P, 8 * TOK])
        sq = norm_work[:, 0:4 * TOK].rearrange("p (s t) -> p s t", t=TOK)
        rt = norm_work[:, 4 * TOK:8 * TOK].rearrange("p (s t) -> p s t", t=TOK)
        a_ = norm_work[:, 0:2 * A_COLS].rearrange("p (e t) -> p e t", t=A_COLS)
        ps_ = sb("pair_scalars", [P, 6, NT + 1, 2])
        glp = sb("state_decay", [P, NT + 1])
        cwp = sb("conv_taps", [P, 3, 4])
        conv_work = sb("conv_work", [P, 4 * TOK])
        conv = conv_work[:, 0:3 * TOK].rearrange("p (w t) -> p w t", t=TOK)
        sp_ = conv_work[:, 0:2 * SEQ].rearrange("p (s t) -> p s t", t=SEQ)
        acc = conv_work[:, 2 * SEQ:4 * SEQ].rearrange("p (s t) -> p s t", t=SEQ)
        act_ = sb("conv_act", [P, 3, TOK])
        qn, kn = sb("qn", [P, SEQ]), sb("kn", [P, TOK])
        kq = sb("kq", [P, NT + 1, 2, P])
        qd = sb("q_decayed", [P, NT + 1, P])
        egr = sb("exp_g_row", [P, NT + 1, P])
        vv = sb("vv", [P, NT + 1, P])
        kbg, ktl, vb = (sb(name, [P, NT + 1, P]) for name in ("kbg", "k_tail", "v_beta"))
        spare = c["h"][:, :, :].rearrange("p m t -> p (m t)")
        rows_end, ys_end = (NT + 1) * 4 * P, (NT + 1) * 6 * P
        rows_in = spare[:, 0:rows_end].rearrange("p (n s t) -> p n s t", s=4, t=P)
        dt_ = sb("decay", [P, NT + 1, 2, P])
        brm = sb("beta_rows", [P, NT + 1, 2, P])
        mtat = sb("mtat", [P, NT + 1, 2, 2, P])
        ml = sb("level_mt", [P, 2, NT + 1, 2, P])
        xx = sb("inverse", [P, NT + 1, 2, 2, P])
        ys = spare[:, rows_end:ys_end].rearrange("p (n s t) -> p n s t", s=2, t=P)
        wt = egr
        vns = sb("v_new", [P, NT + 1, P])
        state = sb("state", [P, NT + 1, HD])
        os_, zs = sb("o_raw", [P, SEQ]), sb("z_silu", [P, SEQ])
        az = sb("abs_z", [P, 2, SEQ])
        bank = own.enter_context(nc.psum_tensor("psB", [P, 8, 512], F32))
        names = """scalars_ready taps_ready convolved silued squares norm_sums roots normed qk_ready transposed
            kv_ready rows_ready vv_ready grown decay_arg beta_ready row_exp decay_exp decay_masked kk kk_used
            mt_ready qd_ready level_ready xt_ready x_transposed x_ready y_ready y_copied x_products x_updated wt_ready
            wt_copied v_new_ready v_new_copied o_ready state_product state_ready o_copied o_squared o_sum o_root
            z_ready o_recip z_scores z_ln z_soft z_masked later_ready cumulated att_exp att_masked att_out
            att_stored pair_done o_normed att_inputs""".split()
        S = {name: sem(name) for name in names}
        act_steps, dve_steps, pool_steps = sem("actB_steps"), sem("dveB_steps"), sem("poolB_steps")
        block = own.enter_context(nc.Block())
        small = c["small"]
        gq, gk, gdn = small[:, 16:17], small[:, 17:18], small[:, 18:19]
        proj, qz, v, scalars, mixed = c["proj"], c["qz"], c["v"], c["scalars"], c["mixed"]
        PER = dict(scalars_ready=1, taps_ready=1, convolved=3, silued=3, squares=4, norm_sums=4, roots=4, normed=4,
                   qk_ready=1, transposed=1, kv_ready=1, rows_ready=1, vv_ready=1, grown=5, decay_arg=5, beta_ready=5,
                   row_exp=4, decay_exp=5, decay_masked=5, kk=5, kk_used=5, mt_ready=5, qd_ready=1,
                   level_ready=len(LEVEL_TILES), xt_ready=5, x_transposed=5, x_ready=5, y_ready=len(STEP_TILES),
                   y_copied=len(STEP_TILES), x_products=len(STEP_TILES), x_updated=len(STEP_TILES), wt_ready=1,
                   wt_copied=1, v_new_ready=5, v_new_copied=5, o_ready=1, state_product=4, state_ready=4, o_copied=1,
                   o_squared=1, o_sum=1, o_root=1, z_ready=1, z_scores=10, z_ln=10, z_soft=10,
                   z_masked=8, later_ready=8, cumulated=10, att_exp=10, att_masked=8, att_out=1, att_stored=1,
                   o_recip=1, o_normed=1, att_inputs=1)
        inc = lambda ins, name, by=1: ins.then_inc(S[name], by)

        def waiter(eng, i):

            def wait(name, k, alone=False):
                if alone:
                    wait_alone(eng, S[name], i * PER[name] + k)
                else:
                    eng.wait_ge(S[name], i * PER[name] + k)

            return wait

        def kk_bank(n):
            return 6 if n % 2 else 2

        def mask_att(pool, wait, a):
            e, kb = ATT[a]
            if kb == 0:
                return
            wait("att_exp", a + 1, alone=True)
            part = a_[:, e, A_OFF[kb]:A_OFF[kb] + P]
            inc(nc.gpsimd.affine_select(out=part, in_=part, compare_op=ALU.is_gt, fill=0.0, base=0,
                                        pattern=[[1, P]], channel_multiplier=-1), "att_masked")

        def last_level(l, n):
            return l == LEVELS - 1 or (n == 0 and l == 3)

        def end_of_pair(eng, i):
            eng.wait_ge(S["pair_done"], i * 4 + 4)

        @block.gpsimd
        def _(pool):
            with pool.Fori(0, PAIRS) as i:
                wait = waiter(pool, i)
                turn = Turn(pool, pool_steps)
                nc.gpsimd.tensor_copy(vv[:, 1:, :], v[:, 1:, bass.ds(i * P, P)])
                inc(nc.gpsimd.tensor_copy(vv[0:META, 0, :], v[0:META, 0, bass.ds(i * P, P)]), "vv_ready")
                wait("scalars_ready", 1)
                for slot, mask, kind in ((0, "tri", 0), (2, "ident", 1)):
                    for rows, cols, n0, n1 in ((P, P, 1, NT + 1), (META, META, 0, 1)):
                        for n in range(n0, n1):
                            last = nc.gpsimd.tensor_tensor(
                                rows_in[0:rows, n, slot:slot + 2, 0:cols], both(c[mask][0:rows, 0:cols], 2),
                                ps_[0:rows, kind, n, :].rearrange("p (e a) -> p e a", a=1).broadcast_to([rows, 2, cols]),
                                ALU.mult)
                inc(last, "rows_ready")
                for n in range(NT + 1):
                    r = tile_rows(n)
                    wait("decay_exp", n + 1, alone=True)
                    inc(nc.gpsimd.affine_select(out=dt_[0:r, n, :, 0:r], in_=dt_[0:r, n, :, 0:r], compare_op=ALU.is_ge,
                                                fill=0.0, base=0, pattern=[[0, 2], [1, r]], channel_multiplier=-1),
                        "decay_masked")
                for n in range(NT + 1):
                    r = tile_rows(n)
                    wait("kk_used", n + 1)
                    wait("beta_ready", n + 1)
                    inc(nc.gpsimd.tensor_tensor(mtat[0:r, n, :, 0, 0:r], mtat[0:r, n, :, 0, 0:r], brm[0:r, n, :, 0:r],
                                                ALU.mult), "mt_ready")

                def level(l):
                    for n in range(NT + 1):
                        if (l, n) not in LEVEL_TILES:
                            continue
                        r = tile_rows(n)
                        if l == 0:
                            wait("mt_ready", n + 1)
                        if l >= 3:
                            wait("y_ready", STEP_TILES.index((l - 2, n)) + 1)
                        if l == 2:
                            wait("xt_ready", n + 1)
                        inc(nc.gpsimd.tensor_tensor(ml[0:r, l % 2, n, :, 0:r], mtat[0:r, n, :, 0, 0:r],
                                                    both(c["levels"][0:r, l, 0:r], 2), ALU.mult), "level_ready")

                level(0)
                level(1)
                for unit, a in UNITS:
                    if unit == "level" and a + 1 < LEVELS:
                        level(a + 1)
                    if unit == "soft" and ATT[a][1] > 0:
                        e, kb = ATT[a]
                        q0 = first_query(kb)
                        d = DIAG.index((e, kb))
                        wait("z_soft", a + 1, alone=True)
                        inc(nc.gpsimd.affine_select(out=sp_[:, a % 2, q0:q0 + P], in_=sp_[:, a % 2, q0:q0 + P],
                                                    compare_op=ALU.is_gt, fill=0.0, base=0, pattern=[[1, P]],
                                                    channel_multiplier=-1), "z_masked")
                        if a >= 2:
                            wait("cumulated", a)
                        wait("z_masked", d + 1, alone=kb == NT)
                        if kb < NT:
                            wait("later_ready", d)
                            nc.gpsimd.tensor_tensor(acc[:, a % 2, q0 + P:], acc[:, (a - 1) % 2, q0 + P:],
                                                    sp_[:, a % 2, q0 + P:], ALU.add)
                        inc(nc.gpsimd.tensor_copy(acc[:, a % 2, q0:q0 + P], sp_[:, a % 2, q0:q0 + P]), "later_ready")
                    if unit == "cum":
                        mask_att(pool, wait, a)
                inc(nc.gpsimd.nop(), "pair_done")
                end_of_pair(pool, i)

        @block.scalar
        def _(act):
            with act.Fori(0, PAIRS) as i:
                wait = waiter(act, i)
                turn = Turn(act, act_steps)
                turn.base = i * 20
                row = lambda t, at: t[:, bass.ds(at, 1), :].rearrange("p a t -> p (a t)")

                def root(s):
                    wait("norm_sums", s + 1)
                    scale = 1.0 / HD if s < 2 else 1.0
                    last = nc.scalar.activation(rt[:, s, META:], bank[:, s, :], ACT.Sqrt, bias=c["eps"][:, :], scale=scale)
                    if s % 2:
                        last = nc.scalar.activation(rt[:, s, 0:META], bank[:, 6 + s // 2, 0:META], ACT.Sqrt,
                                                    bias=c["eps"][:, :], scale=scale)
                    inc(last, "roots")

                inc(nc.scalar.activation(sq[:, 0, META:], row(qz, i), ACT.Square), "squares")
                inc(nc.scalar.activation(sq[:, 1, :], row(proj, i), ACT.Square), "squares")
                root(0)
                root(1)
                for w in range(3):
                    wait("convolved", w + 1)
                    inc(nc.scalar.activation(act_[:, w, :], conv[:, w, :], ACT.Silu), "silued")
                wait("silued", 2)
                for w in range(2):
                    inc(nc.scalar.activation(sq[:, 2 + w, :], act_[:, w, :], ACT.Square), "squares")
                inc(nc.scalar.activation(zs[:, :], row(qz, i + PAIRS), ACT.Silu), "z_ready")
                root(2)
                root(3)
                for n in range(NT + 1):
                    r = tile_rows(n)
                    wait("beta_ready", n + 1)
                    if n > 0:
                        for e in range(2):
                            h = slice(e * HD, (e + 1) * HD)
                            last = nc.scalar.activation(egr[h, n, :], bank[h, n % 2, e * P:(e + 1) * P], ACT.Exp)
                        inc(last, "row_exp")
                    wait("decay_arg", n + 1)
                    inc(nc.scalar.activation(dt_[0:r, n, :, 0:r], dt_[0:r, n, :, 0:r], ACT.Exp), "decay_exp")
                for n in range(NT + 1):
                    r = tile_rows(n)
                    wait("x_transposed", n + 1)
                    inc(nc.scalar.activation(xx[0:r, n, :, 0, 0:r], bank[0:r, 4 + n % 2, 0:2 * r].rearrange(
                        "p (e c) -> p e c", e=2), ACT.Copy), "x_ready")
                for unit, a in UNITS:
                    if unit == "level":
                        for n in range(NT + 1):
                            if (a, n) not in STEP_TILES:
                                continue
                            t, r = STEP_TILES.index((a, n)), tile_rows(n)
                            wait("y_ready", t + 1)
                            inc(nc.scalar.activation(ys[0:r, n, :, 0:r], bank[0:r, 4 + t % 2, 0:2 * r].rearrange(
                                "p (e c) -> p e c", e=2), ACT.Copy), "y_copied")
                    elif unit == "z":
                        e, kb = ATT[a]
                        r, q0 = tile_rows(kb), first_query(kb)
                        part = az[0:r, a % 2, q0:]
                        if a >= 2:
                            wait("z_soft", a - 1)
                        wait("z_scores", a + 1)
                        turn.then(nc.scalar.activation(part, bank[0:r, a % 2, q0:], ACT.Abs))
                        turn.then(nc.scalar.activation(part, part, ACT.Exp, scale=-1.0))
                        inc(nc.scalar.activation(part, part, ACT.Ln, bias=c["ones"][0:r, 0:1]), "z_ln")
                    elif unit == "cum":
                        e, kb = ATT[a]
                        r, q0 = tile_rows(kb), first_query(kb)
                        wait("cumulated", a + 1)
                        inc(nc.scalar.activation(a_[0:r, e, A_OFF[kb]:A_OFF[kb] + SEQ - q0], bank[0:r, a % 2, q0:],
                                                 ACT.Exp), "att_exp")
                wait("wt_ready", 1)
                inc(nc.scalar.activation(wt[:, 1:, :], bank[:, 4, :].rearrange("p (n c) -> p n c", c=P), ACT.Copy),
                    "wt_copied")
                for n in range(NT + 1):
                    r = tile_rows(n)
                    wait("v_new_ready", n + 1)
                    inc(nc.scalar.activation(vns[0:r, n, :].rearrange("p (e d) -> p e d", e=2),
                                             bank[0:r, 6:8, 0:HD], ACT.Copy), "v_new_copied")
                wait("o_copied", 1)
                inc(nc.scalar.activation(sq[:, 0, 0:SEQ], os_[:, :], ACT.Square), "o_squared")
                wait("o_sum", 1)
                inc(nc.scalar.activation(rt[:, 0, 0:SEQ], bank[:, 3, :], ACT.Sqrt, bias=c["eps"][:, :],
                                         scale=1.0 / HD), "o_root")
                inc(nc.scalar.nop(), "pair_done")
                end_of_pair(act, i)

        @block.vector
        def _(dve):
            with dve.Fori(0, PAIRS) as i:
                wait = waiter(dve, i)
                turn = Turn(dve, dve_steps)
                row = lambda t, at: t[:, bass.ds(at, 1), :].rearrange("p a t -> p (a t)")
                inc(nc.vector.tensor_copy(ps_[:, :, :, :].rearrange("p k n e -> p (k n) e"),
                                          scalars[:, :, :, bass.ds(i * 2, 2)].rearrange("p k n e -> p (k n) e")),
                    "scalars_ready")
                inc(nc.vector.tensor_copy(cwp[:, :, :], c["conv_w"][:, :, bass.ds(i, 1), :].rearrange(
                    "p w a j -> p w (a j)")), "taps_ready")
                wait("scalars_ready", 1)
                for e in range(2):
                    h = slice(e * HD, (e + 1) * HD)
                    nc.vector.tensor_copy(glp[h, :], ps_[h, 5, :, e])
                wait("taps_ready", 1)
                for j in range(3, -1, -1):
                    for w in range(3):
                        raw, s = row(proj, i + (w + 1) * PAIRS), 3 - j
                        tap = cwp[:, w, j:j + 1]
                        if s == 0:
                            turn(nc.vector.tensor_scalar(conv[:, w, :], raw, tap, None, ALU.mult))
                            continue
                        dve.wait_ge(dve_steps, i * 9 + (s - 1) * 3 + w + 1)
                        last = nc.vector.scalar_tensor_tensor(out=conv[:, w, s:], in0=raw[:, 0:TOK - s], scalar=tap,
                                                              in1=conv[:, w, s:], op0=ALU.mult, op1=ALU.add)
                        if j == 0:
                            inc(last, "convolved")
                        else:
                            turn(last)
                assert turn.count == 9

                def norm(s):
                    lo = 0 if s % 2 else META
                    wait("roots", s + 1)
                    inc(nc.vector.reciprocal(rt[:, s, lo:], rt[:, s, lo:]), "normed")

                def grow_rows(n):
                    r = tile_rows(n)
                    wait("grown", n + 1)
                    grow = bank[0:r, n % 2, 0:4 * r].rearrange("p (k c) -> p k c", k=4)
                    for e in range(2):
                        last = nc.vector.tensor_scalar(dt_[0:r, n, e, 0:r], grow[:, e, :], ps_[0:r, 2, n, e:e + 1], 0.0,
                                                       ALU.subtract, ALU.min)
                    inc(last, "decay_arg")
                    inc(nc.vector.tensor_tensor(brm[0:r, n, :, 0:r], grow[:, 2:4, :], both(c["strict"][0:r, 0:r], 2),
                                                ALU.mult), "beta_ready")

                grow_rows(0)
                grow_rows(1)
                norm(0)
                norm(2)
                norm(3)
                wait("normed", 3)
                tiles = lambda ap: ap.rearrange("p (n c) -> p n c", c=P)
                nc.vector.scalar_tensor_tensor(out=kq[:, 1:, 1, :], in0=tiles(act_[:, 0, META:]), scalar=HD ** -0.5,
                                               in1=tiles(rt[:, 2, META:]), op0=ALU.mult, op1=ALU.mult)
                nc.vector.tensor_tensor(kq[:, 1:, 0, :], tiles(act_[:, 1, META:]), tiles(rt[:, 3, META:]), ALU.mult)
                inc(nc.vector.tensor_tensor(kq[:, 0, 0, 0:META], act_[:, 1, 0:META], rt[:, 3, 0:META], ALU.mult),
                    "qk_ready")
                for n in range(2, NT + 1):
                    grow_rows(n)
                wait("transposed", 1)
                for out, src, kind in ((kbg, 4, 3), (ktl, 4, 4), (vb, 5, 1)):
                    nc.vector.tensor_tensor(
                        out[:, 1:, :].rearrange("p n (e d) -> p n e d", e=2),
                        bank[:, src, :].rearrange("p (n e d) -> p n e d", e=2, d=HD),
                        ps_[:, kind, 1:, :].rearrange("p n (e a) -> p n e a", a=1).broadcast_to([P, NT, 2, HD]), ALU.mult)
                for out, src, kind in ((ktl, 0, 4), (vb, P, 1)):
                    last = nc.vector.tensor_tensor(
                        out[0:META, 0, :].rearrange("p (e d) -> p e d", e=2),
                        bank[0:META, 6, src:src + P].rearrange("p (e d) -> p e d", e=2),
                        ps_[0:META, kind, 0, :].rearrange("p (e a) -> p e a", a=1).broadcast_to([META, 2, HD]), ALU.mult)
                inc(last, "kv_ready")
                for n in range(NT + 1):
                    r, w = tile_rows(n), 2 if n else 1
                    wait("kk", n + 1)
                    wait("decay_masked", n + 1)
                    inc(nc.vector.tensor_tensor(
                        mtat[0:r, n, :, 0:w, 0:r],
                        bank[0:r, kk_bank(n):kk_bank(n) + 2, 0:w * r].rearrange("p e (w c) -> p e w c", w=w),
                        dt_[0:r, n, :, 0:r].rearrange("p e (a c) -> p e a c", a=1).broadcast_to([r, 2, w, r]), ALU.mult),
                        "kk_used")
                wait("row_exp", 4)
                inc(nc.vector.tensor_tensor(qd[:, 1:, :], kq[:, 1:, 1, :], egr[:, 1:, :], ALU.mult), "qd_ready")
                norm(1)
                wait("normed", 4)
                nc.vector.scalar_tensor_tensor(out=qn[:, :], in0=row(qz, i), scalar=gq, in1=rt[:, 0, META:],
                                               op0=ALU.mult, op1=ALU.mult)
                inc(nc.vector.scalar_tensor_tensor(out=kn[:, :], in0=row(proj, i), scalar=gk, in1=rt[:, 1, :],
                                                   op0=ALU.mult, op1=ALU.mult), "att_inputs")
                for n in range(NT + 1):
                    r = tile_rows(n)
                    wait("level_ready", n + 1)
                    inc(nc.vector.tensor_tensor(xx[0:r, n, :, 1, 0:r], both(c["ident"][0:r, 0:r], 2),
                                                ml[0:r, 0, n, :, 0:r], ALU.subtract), "xt_ready")
                for unit, a in UNITS:
                    if unit == "products":
                        for n in range(NT + 1):
                            if (a, n) not in STEP_TILES:
                                continue
                            t, r = STEP_TILES.index((a, n)), tile_rows(n)
                            w0 = 1 if last_level(a, n) else 0
                            wait("x_products", t + 1)
                            part = xx[0:r, n, :, w0:, 0:r]
                            inc(nc.vector.tensor_tensor(part, part, bank[0:r, 6 + t % 2, 0:4 * r].rearrange(
                                "p (e w c) -> p e w c", e=2, w=2)[:, :, w0:, :], ALU.subtract), "x_updated")
                    elif unit == "soft":
                        e, kb = ATT[a]
                        r, q0 = tile_rows(kb), first_query(kb)
                        wait("z_ln", a + 1)
                        if a >= 2:
                            wait("cumulated", a - 1)
                            wait("later_ready", len([x for x in ATT[:a - 1] if x[1] > 0]))
                        inc(nc.vector.scalar_tensor_tensor(out=sp_[0:r, a % 2, q0:], in0=bank[0:r, a % 2, q0:], scalar=0.0,
                                                           in1=az[0:r, a % 2, q0:], op0=ALU.max, op1=ALU.add), "z_soft")
                    elif unit == "pv" and a == 1:
                        wait("att_out", 1)
                        inc(nc.vector.tensor_copy(row(mixed, i), bank[:, 2, :]), "att_stored")
                for n in range(NT):
                    wait("state_product", n + 1)
                    if n == 0:
                        inc(nc.vector.tensor_copy(state[:, 1, :], bank[:, 3, 0:HD]), "state_ready")
                        continue
                    wait("state_ready", n)
                    inc(nc.vector.scalar_tensor_tensor(out=state[:, n + 1, :], in0=state[:, n, :], scalar=glp[:, n:n + 1],
                                                       in1=bank[:, 3, 0:HD], op0=ALU.mult, op1=ALU.add), "state_ready")
                wait("o_ready", 1)
                inc(nc.vector.tensor_copy(os_[:, :], bank[:, 5, :]), "o_copied")
                wait("o_root", 1)
                inc(nc.vector.reciprocal(rt[:, 0, 0:SEQ], rt[:, 0, 0:SEQ]), "o_recip")
                wait("o_recip", 1)
                inc(nc.vector.scalar_tensor_tensor(out=os_[:, :], in0=os_[:, :], scalar=gdn, in1=rt[:, 0, 0:SEQ],
                                                   op0=ALU.mult, op1=ALU.mult), "o_normed")
                wait("o_normed", 1)
                wait("z_ready", 1)
                nc.vector.tensor_tensor(row(mixed, i + PAIRS), os_[:, :], zs[:, :], ALU.mult).then_inc(S["pair_done"], 1)
                end_of_pair(dve, i)

        @block.tensor
        def _(pe):
            mm = nc.tensor.matmul
            with pe.Fori(0, PAIRS) as i:
                wait = waiter(pe, i)
                half = lambda e: slice(e * HD, (e + 1) * HD)

                def square_sums(s):
                    wait("squares", s + 1)
                    last = mm(bank[:, s, :], c["blocks"][:, :], sq[:, s, META:], start=True, stop=True)
                    if s % 2:
                        last = mm(bank[:, 6 + s // 2, 0:META], c["blocks"][:, :], sq[:, s, 0:META], start=True,
                                  stop=True)
                    inc(last, "norm_sums")

                def grow(n):
                    r = tile_rows(n)
                    if n >= 2:
                        wait("beta_ready", n - 1)
                        wait("row_exp", n - 2) if n > 2 else None
                    inc(mm(bank[:, n % 2, 0:4 * r].rearrange("p (k c) -> p k c", k=4), c["ones"][0:r, :],
                           rows_in[0:r, n, :, 0:r], start=True, stop=True), "grown")

                square_sums(0)
                square_sums(1)
                wait("rows_ready", 1)
                wait("roots", 2)
                grow(0)
                grow(1)
                square_sums(2)
                square_sums(3)
                for n in range(2, NT + 1):
                    grow(n)
                wait("qk_ready", 1)
                wait("silued", 3)
                for n in range(1, NT + 1):
                    lo, hi = tile_cols(n)
                    nc.tensor.transpose(bank[:, 4, (n - 1) * P:n * P], kq[:, n, 0, :], c["ident"][:, :])
                    nc.tensor.transpose(bank[:, 5, (n - 1) * P:n * P], act_[:, 2, lo:hi], c["ident"][:, :])
                nc.tensor.transpose(bank[0:META, 6, 0:P], kq[:, 0, 0, 0:META], c["ident"][:, :])
                inc(nc.tensor.transpose(bank[0:META, 6, P:2 * P], act_[:, 2, 0:META], c["ident"][:, :]), "transposed")
                wait("kv_ready", 1, alone=True)
                for n in range(NT + 1):
                    r, w = tile_rows(n), 2 if n else 1
                    if n >= 2:
                        wait("kk_used", n - 1)
                    for e in range(2):
                        last = mm(bank[0:r, kk_bank(n) + e, 0:w * r].rearrange("p (w c) -> p w c", w=w),
                                  kq[half(e), n, 0, 0:r], kq[half(e), n, 0:w, 0:r], start=True, stop=True)
                    inc(last, "kk")
                for n in range(NT + 1):
                    r = tile_rows(n)
                    if n >= 2:
                        wait("x_ready", n - 1)
                    wait("xt_ready", n + 1, alone=n == 0)
                    for e in range(2):
                        last = nc.tensor.transpose(bank[0:r, 4 + n % 2, e * r:(e + 1) * r], xx[0:r, n, e, 1, 0:r],
                                                   c["ident"][0:r, 0:r])
                    inc(last, "x_transposed")
                for unit, a in UNITS:
                    tiles = [n for n in range(NT + 1) if (a, n) in STEP_TILES]
                    if unit == "level":
                        for n in tiles:
                            t, r = STEP_TILES.index((a, n)), tile_rows(n)
                            wait("level_ready", LEVEL_TILES.index((a, n)) + 1, alone=n == 0)
                            if a == 1:
                                wait("x_ready", NT + 1)
                            else:
                                wait("x_updated", STEP_TILES.index((a - 1, n)) + 1)
                            if t >= 2:
                                wait("y_copied", t - 1)
                            for e in range(2):
                                last = mm(bank[0:r, 4 + t % 2, e * r:(e + 1) * r], ml[0:r, a % 2, n, e, 0:r],
                                          xx[0:r, n, e, 0, 0:r], start=True, stop=True)
                            inc(last, "y_ready")
                    elif unit == "products":
                        for n in tiles:
                            t, r = STEP_TILES.index((a, n)), tile_rows(n)
                            wait("y_copied", t + 1, alone=n == 0)
                            if t >= 2:
                                wait("x_updated", t - 1)
                            for e in range(2):
                                b = 6 + t % 2
                                if not last_level(a, n):
                                    mm(bank[0:r, b, 2 * e * r:(2 * e + 1) * r], xx[0:r, n, e, 1, 0:r],
                                       ys[0:r, n, e, 0:r], start=True, stop=True)
                                last = mm(bank[0:r, b, (2 * e + 1) * r:(2 * e + 2) * r], ys[0:r, n, e, 0:r],
                                          xx[0:r, n, e, 1, 0:r], start=True, stop=True)
                            inc(last, "x_products")
                    elif unit == "z":
                        e, kb = ATT[a]
                        r, q0 = tile_rows(kb), first_query(kb)
                        lo, hi = tile_cols(kb)
                        if a == 0:
                            wait("att_inputs", 1)
                        if a >= 2:
                            wait("att_exp", a - 1, alone=kb == 0)
                        inc(mm(bank[0:r, a % 2, q0:], kn[half(e), lo:hi], qn[half(e), q0:], start=True, stop=False,
                               skip_group_check=True), "z_scores")
                    elif unit == "cum":
                        e, kb = ATT[a]
                        r, q0 = tile_rows(kb), first_query(kb)
                        if kb:
                            wait("z_masked", DIAG.index((e, kb)) + 1)
                        else:
                            wait("z_soft", a + 1, alone=True)
                        last = mm(bank[0:r, a % 2, q0:], c["neglow"][0:r, 0:r], sp_[0:r, a % 2, q0:], start=False,
                                  stop=kb == NT, skip_group_check=True)
                        if kb < NT:
                            later = q0 + P if kb else 0
                            wait("later_ready", DIAG.index(ATT[a - 1]) + 1)
                            last = mm(bank[0:r, a % 2, later:], c["negones"][:, 0:r], acc[:, (a - 1) % 2, later:],
                                      start=False, stop=True, skip_group_check=True)
                        inc(last, "cumulated")
                    elif unit == "pv":
                        e = a
                        wait("att_exp", 5 * e + 5)
                        wait("att_masked", 4 * e + 4)
                        wait("vv_ready", 1)
                        for kb in range(NT + 1):
                            r, q0 = tile_rows(kb), first_query(kb)
                            last = mm(bank[half(e), 2, q0:], vv[0:r, kb, half(e)],
                                      a_[0:r, e, A_OFF[kb]:A_OFF[kb] + SEQ - q0], start=kb == 0, stop=kb == NT)
                        if e == 1:
                            inc(last, "att_out")
                wait("x_updated", len(STEP_TILES))
                for n in range(1, NT + 1):
                    for e in range(2):
                        last = mm(bank[half(e), 4, (n - 1) * P:n * P], kbg[:, n, half(e)], xx[:, n, e, 1, :], start=True,
                                  stop=True)
                inc(last, "wt_ready")
                for n in range(NT + 1):
                    r = tile_rows(n)
                    if n == 1:
                        wait("wt_copied", 1)
                        wait("qd_ready", 1)
                    if n:
                        wait("state_ready", n)
                    for e in range(2):
                        last = mm(bank[0:r, 6 + e, 0:HD], xx[0:r, n, e, 1, 0:r], vb[0:r, n, half(e)], start=True,
                                  stop=n == 0)
                        if n:
                            last = mm(bank[0:r, 6 + e, 0:HD], wt[half(e), n, :], state[half(e), n, :], start=False,
                                      stop=True)
                    inc(last, "v_new_ready")
                    wait("v_new_copied", n + 1, alone=n == NT)
                    if n < NT:
                        for e in range(2):
                            last = mm(bank[half(e), 3, 0:HD], ktl[0:r, n, half(e)], vns[0:r, n, half(e)], start=True,
                                      stop=True)
                        inc(last, "state_product")
                    if n:
                        for e in range(2):
                            o = bank[half(e), 5, (n - 1) * P:n * P]
                            mm(o, state[half(e), n, :], qd[half(e), n, :], start=True, stop=False)
                            last = mm(o, vns[:, n, half(e)], mtat[:, n, e, 1, :], start=False, stop=True)
                inc(last, "o_ready")
                wait("o_squared", 1)
                inc(mm(bank[:, 3, :], c["blocks"][:, :], sq[:, 0, 0:SEQ], start=True, stop=True), "o_sum")
                wait("att_stored", 1)
                inc(nc.tensor.nop(), "pair_done")
                end_of_pair(pe, i)



def mix_and_add(nc, c, w_mixers, w_o, gates_dram, xT):
    with ExitStack() as own:
        sb = lambda name, shape, dt=F32: c["sb"](own, name, shape, dt)
        sem = lambda name: own.enter_context(nc.semaphore(name))
        oh, ol = sb("oh", [P, DC, SEQ], F32R), sb("ol", [P, DC, SEQ], F32R)
        mh, ml = sb("mh", [P, DC, SEQ], F32R), sb("ml", [P, DC, SEQ], F32R)
        ring = sb("w_ring2", [P, RING, DC, P])
        ring_h, ring_l = sb("ring_h2", [P, RING, DC, P], F32R), sb("ring_l2", [P, RING, DC, P], F32R)
        gates = sb("gates", [P, 2, 2, SEQ])
        parts = sb("gated_parts", [P, 2, 2, SEQ])
        x = sb("x_rows", [P, 2, SEQ])
        mixer_out, h = c["mixed"], c["h"]
        ps = own.enter_context(nc.psum_tensor("psC", [P, 8, 512], F32))
        st = WeightStream(sem, "out")
        gate_loaded = [c["dma_sem"](f"gate_loaded{s}") for s in range(2)]
        x_loaded = [c["dma_sem"](f"x_again{s}") for s in range(2)]
        o_hi, o_lo, gate_ready, gated, gate_used = (sem(n) for n in ("o_hi", "o_lo", "gate_ready", "gated", "gate_used"))
        mix_ready, mix_hi, mix_lo, x_used = sem("mix_ready"), sem("mix_hi"), sem("mix_lo"), sem("x_used")
        block = own.enter_context(nc.Block())

        @block.sync
        def _(sp):
            for k in range(RING):
                sp.dma_start(ring[:, k, :, :], w_mixers[k]).then_inc(st.loaded[k], 16)
            for r in range(RING):
                sp.wait_ge(st.lo, r + 1)
                sp.dma_start(ring[:, r, :, :], w_mixers[RING + r]).then_inc(st.loaded[r], 16)
            with sp.Fori(0, DC // RING) as i:
                for r in range(RING):
                    sp.wait_ge(st.lo, i * RING + (RING + r + 1))
                    sp.dma_start(ring[:, r, :, :], w_o[bass.ds(i * RING + r, 1)].rearrange(
                        "a p c f -> (a p) c f")).then_inc(st.loaded[r], 16)

        @block.gpsimd
        def _(pool):
            def load(m, slot):
                for g in range(2):
                    pool.dma_start(gates[:, slot, g, :], gates_dram[m + g * DC]).then_inc(gate_loaded[slot], 16)

            for m in range(DC):
                if m >= 2:
                    pool.wait_ge(gate_used, m - 1)
                load(m, m % 2)
            for m in range(DC):
                if m >= 2:
                    pool.wait_ge(x_used, m - 1)
                pool.dma_start(x[:, m % 2, :], xT[m][:, META:]).then_inc(x_loaded[m % 2], 16)

        @block.scalar
        def _(act):
            def hi(k):
                act.wait_ge(st.loaded[k % RING], 16 * (k // RING + 1))
                if k >= RING:
                    act.wait_ge(st.used, k - RING + 1)
                nc.scalar.activation(ring_h[:, k % RING, :, :], ring[:, k % RING, :, :], ACT.Copy).then_inc(st.hi, 1)

            for k in range(DC):
                nc.scalar.activation(oh[:, k, :], mixer_out[:, k, :], ACT.Copy).then_inc(o_hi, 1)
            hi(0)
            hi(1)
            for m in range(DC):
                act.wait_ge(gate_loaded[m % 2], 32 * (m // 2 + 1))
                nc.scalar.activation(gates[:, m % 2, :, :], gates[:, m % 2, :, :], ACT.Sigmoid).then_inc(gate_ready, 1)
                if m >= 1:
                    act.wait_ge(mix_ready, m)
                    nc.scalar.activation(mh[:, m - 1, :], parts[:, (m - 1) % 2, 0, :], ACT.Copy).then_inc(mix_hi, 1)
                hi(m + 2)
            act.wait_ge(mix_ready, DC)
            nc.scalar.activation(mh[:, DC - 1, :], parts[:, (DC - 1) % 2, 0, :], ACT.Copy).then_inc(mix_hi, 1)
            for k in range(DC + 2, 2 * DC):
                hi(k)

        @block.vector
        def _(dve):
            def lo(k):
                dve.wait_ge(st.hi, k + 1)
                nc.vector.tensor_tensor(ring_l[:, k % RING, :, :], ring[:, k % RING, :, :],
                                        ring_h[:, k % RING, :, :].bitcast(F32), ALU.subtract).then_inc(st.lo, 1)

            def mix_low(m):
                dve.wait_ge(mix_hi, m + 1)
                nc.vector.tensor_tensor(ml[:, m, :], parts[:, m % 2, 0, :], mh[:, m, :].bitcast(F32),
                                        ALU.subtract).then_inc(mix_lo, 1)

            for k in range(DC):
                dve.wait_ge(o_hi, k + 1)
                nc.vector.tensor_tensor(ol[:, k, :], mixer_out[:, k, :], oh[:, k, :].bitcast(F32),
                                        ALU.subtract).then_inc(o_lo, 1)
            lo(0)
            lo(1)
            for m in range(DC):
                if m >= 1:
                    mix_low(m - 1)
                dve.wait_ge(st.used, m + 1)
                dve.wait_ge(gate_ready, m + 1)
                b = 2 * (m % 2)
                nc.vector.tensor_tensor(parts[:, m % 2, :, :], gates[:, m % 2, :, :], ps[:, b:b + 2, :],
                                        ALU.mult).then_inc(gate_used, 1)
                dve.wait_ge(gate_used, m + 1)
                nc.vector.tensor_tensor(parts[:, m % 2, 0, :], parts[:, m % 2, 0, :], parts[:, m % 2, 1, :],
                                        ALU.add).then_inc(mix_ready, 1)
                lo(m + 2)
            mix_low(DC - 1)
            for m in range(DC):
                if m + 2 < DC:
                    lo(DC + m + 2)
                dve.wait_ge(st.used, DC + m + 1)
                dve.wait_ge(x_loaded[m % 2], 16 * (m // 2 + 1))
                nc.vector.tensor_tensor(h[:, m, :], x[:, m % 2, :], ps[:, 4 + m % 2, :], ALU.add).then_inc(x_used, 1)

        @block.tensor
        def _(pe):
            pe.wait_ge(o_lo, DC)
            for m in range(2 * DC):
                r = m % RING
                pe.wait_ge(st.lo, m + 1)
                if m < DC:
                    if m >= 2:
                        pe.wait_ge(gate_used, m - 1)
                    for k in range(DC):
                        last = products(nc, ps[:, 2 * (m % 2) + k // 4, :], (ring_h[:, r, k, :], ring_l[:, r, k, :]),
                                        (oh[:, k, :], ol[:, k, :]), k % 4 == 0, k % 4 == 3)
                else:
                    if m == DC:
                        pe.wait_ge(mix_lo, DC)
                    if m >= DC + 2:
                        pe.wait_ge(x_used, m - DC - 1)
                    for k in range(DC):
                        last = products(nc, ps[:, 4 + m % 2, :], (ring_h[:, r, k, :], ring_l[:, r, k, :]),
                                        (mh[:, k, :], ml[:, k, :]), k == 0, k == DC - 1)
                last.then_inc(st.used, 1)


def peer_scores(nc, c, w_q, keys_dram):
    with ExitStack() as own:
        sb = lambda name, shape, dt=F32: c["sb"](own, name, shape, dt)
        sem = lambda name: own.enter_context(nc.semaphore(name))
        work = sb("work2", [P, DC, SEQ])
        rstd = sb("rstd2", [P, SEQ])
        ring = sb("w_ring3", [P, RING, DC, P])
        ring_h, ring_l = sb("ring_h3", [P, RING, DC, P], F32R), sb("ring_l3", [P, RING, DC, P], F32R)
        keys = sb("keys", [P, 2, KEYS])
        query = sb("query", [P, 2, SEQ])
        ps = own.enter_context(nc.psum_tensor("psQ", [P, 8, 512], F32))
        h, xh, xl, scores = c["h"], c["x2h"], c["x2l"], c["scores"]
        st = WeightStream(sem, "query")
        names = "squared2 summed2 rooted2 recip2 normed2 x2_hi x2_lo keys_loaded scored stored".split()
        squared, summed, rooted, recip, normed, x_hi, x_lo, keys_loaded, scored, stored = (sem(n) for n in names)
        block = own.enter_context(nc.Block())
        n = 2 * HEADS

        @block.sync
        def _(sp):
            for k in range(RING):
                sp.dma_start(ring[:, k, :, :], w_q[k]).then_inc(st.loaded[k], 16)
            sp.dma_start(keys[:, :, :], keys_dram).then_inc(keys_loaded, 16)
            with sp.Fori(0, n // RING - 1) as i:
                for r in range(RING):
                    sp.wait_ge(st.lo, i * RING + r + 1)
                    sp.dma_start(ring[:, r, :, :], w_q[bass.ds(i * RING + (RING + r), 1)].rearrange(
                        "a p c f -> (a p) c f")).then_inc(st.loaded[r], 16)

        @block.scalar
        def _(act):
            for k in range(DC):
                nc.scalar.activation(work[:, k, :], h[:, k, :], ACT.Square).then_inc(squared, 1)
            act.wait_ge(summed, 1)
            nc.scalar.activation(rstd[:, :], ps[:, 0, :], ACT.Sqrt, bias=c["eps"][:, :], scale=1.0 / D).then_inc(rooted, 1)
            for k in range(DC):
                act.wait_ge(normed, k + 1)
                nc.scalar.activation(xh[:, k, :], work[:, k, :], ACT.Copy).then_inc(x_hi, 1)

            def hi(slot, loads, used):
                act.wait_ge(st.loaded[slot], loads)
                if used is not None:
                    act.wait_ge(st.used, used)
                nc.scalar.activation(ring_h[:, slot, :, :], ring[:, slot, :, :], ACT.Copy).then_inc(st.hi, 1)

            def store(at, r):
                act.wait_ge(scored, at + r + 1)
                out = scores[:, :, bass.ds(at + r, 1), :].rearrange("p t a k -> p t (a k)")
                nc.scalar.activation(out, ps[:, 4 + r % 2, :].rearrange("p (t k) -> p t k", k=KEYS),
                                     ACT.Copy).then_inc(stored, 1)

            for k in range(RING):
                hi(k, 16, None)
            with act.Fori(0, n // RING - 1) as i:
                for r in range(RING):
                    hi(r, i * 16 + 32, i * RING + r + 1)
                    store(i * RING, r)
            for r in range(RING):
                store(n - RING, r)

        @block.vector
        def _(dve):
            dve.wait_ge(rooted, 1)
            nc.vector.reciprocal(rstd[:, :], rstd[:, :]).then_inc(recip, 1)
            dve.wait_ge(recip, 1)
            for k in range(DC):
                nc.vector.scalar_tensor_tensor(out=work[:, k, :], in0=h[:, k, :], scalar=c["small"][:, 19 + k:20 + k],
                                               in1=rstd[:, :], op0=ALU.mult, op1=ALU.mult).then_inc(normed, 1)
            for k in range(DC):
                dve.wait_ge(x_hi, k + 1)
                nc.vector.tensor_tensor(xl[:, k, :], work[:, k, :], xh[:, k, :].bitcast(F32),
                                        ALU.subtract).then_inc(x_lo, 1)

            def lo(slot, his):
                dve.wait_ge(st.hi, his)
                nc.vector.tensor_tensor(ring_l[:, slot, :, :], ring[:, slot, :, :],
                                        ring_h[:, slot, :, :].bitcast(F32), ALU.subtract).then_inc(st.lo, 1)

            def take(at, r):
                dve.wait_ge(st.used, at + r + 1)
                nc.vector.tensor_copy(query[:, r % 2, :], ps[:, 2 + r % 2, :]).then_inc(st.evacuated, 1)

            lo(0, 1)
            lo(1, 2)
            for r in range(RING):
                lo((r + 2) % RING, r + 3)
                if r >= 2:
                    dve.wait_ge(scored, r - 1)
                take(0, r)
            with dve.Fori(1, n // RING - 1) as i:
                for r in range(RING):
                    lo((r + 2) % RING, i * RING + r + 3)
                    dve.wait_ge(scored, i * RING + r - 1)
                    take(i * RING, r)
            for r in range(RING):
                if r < RING - 2:
                    lo((r + 2) % RING, n - RING + r + 3)
                dve.wait_ge(scored, n - RING + r - 1)
                take(n - RING, r)

        @block.tensor
        def _(pe):
            for k in range(DC):
                pe.wait_ge(squared, k + 1)
                last = nc.tensor.matmul(ps[:, 0, :], c["ones"][:, :], work[:, k, :], start=k == 0, stop=k == DC - 1)
            last.then_inc(summed, 1)
            pe.wait_ge(x_lo, DC)
            pe.wait_ge(keys_loaded, 16)

            def project(k, slot):
                pe.wait_ge(st.lo, k + 1)
                for ch in range(DC):
                    last = products(nc, ps[:, 2 + slot % 2, :], (ring_h[:, slot, ch, :], ring_l[:, slot, ch, :]),
                                    (xh[:, ch, :], xl[:, ch, :]), ch == 0, ch == DC - 1)
                last.then_inc(st.used, 1)

            def score(k, slot):
                pe.wait_ge(st.evacuated, k + 1)
                for t in range(NT):
                    last = nc.tensor.matmul(ps[:, 4 + slot % 2, t * P:(t + 1) * P],
                                            query[:, slot % 2, t * P:(t + 1) * P], keys[:, slot % 2, :], start=True,
                                            stop=True)
                last.then_inc(scored, 1)

            for r in range(RING):
                if r >= 2:
                    pe.wait_ge(st.evacuated, r - 1)
                project(r, r)
                if r >= 1:
                    if r >= 3:
                        pe.wait_ge(stored, r - 2)
                    score(r - 1, r - 1)
            with pe.Fori(1, n // RING) as i:
                for r in range(RING):
                    pe.wait_ge(st.evacuated, i * RING + (r - 1))
                    project(i * RING + r, r)
                    pe.wait_ge(stored, i * RING + (r - 2))
                    score(i * RING + (r - 1), (r - 1) % RING)
            pe.wait_ge(stored, n - 2)
            score(n - 1, RING - 1)


def route(nc, c):
    with ExitStack() as own:
        sb = lambda name, shape, dt=F32: c["sb"](own, name, shape, dt)
        sem = lambda name: own.enter_context(nc.semaphore(name))
        s = sb("tile_scores", [P, 2 * HEADS, KEYS])
        val = sb("half_best", [P, HEADS, 2, TOPK])
        idx = sb("half_index", [P, HEADS, 2, TOPK], U32)
        idxf = sb("half_index_f", [P, HEADS, 2, TOPK])
        cand = sb("candidates", [P, HEADS, TOPK * TOPK])
        match = sb("rank_match", [P, 2, HEADS, TOPK * TOPK])
        top, pos = sb("top", [P, HEADS, TOPK]), sb("top_position", [P, HEADS, TOPK], U32)
        rank = sb("half_rank", [P, 2, HEADS, TOPK], U32)
        rankf = sb("half_rank_f", [P, 2, HEADS, TOPK])
        picked = sb("picked", [P, 3, HK])
        total = sb("gate_total", [P, HEADS])
        whole = sb("gate_whole", [P, P])
        part16 = sb("gate_part", [P, P], F16)
        ps = own.enter_context(nc.psum_tensor("psR", [P, 512], F32))
        ranks_done = sem("rank_steps")
        steps, copied, shifted, exped, turned, taken, picked_done = (
            sem(n) for n in ("route_steps", "scores_copied", "top_shifted", "top_exped", "picked_turned", "picked_taken",
                             "picked_ready"))
        block = own.enter_context(nc.Block())
        routed = c["routed"]
        STEPS = 13

        @block.scalar
        def _(act):
            with act.Fori(0, NT) as i:
                nc.scalar.activation(s[:, :, :], c["scores"][:, bass.ds(i, 1), :, :].rearrange("p a h k -> p (a h) k"),
                                     ACT.Copy).then_inc(copied, 1)
                act.wait_ge(shifted, i + 1)
                gate = picked[:, 2, :]
                nc.scalar.activation(gate, gate, ACT.Exp).then_inc(exped, 1)
                act.wait_ge(taken, i + 1)

        @block.tensor
        def _(pe):
            with pe.Fori(0, NT) as i:
                pe.wait_ge(picked_done, i + 1)
                for k in range(3):
                    last = nc.tensor.transpose(ps[:, k * P:(k + 1) * P], picked[:, k, :], c["ident"][:, :])
                last.then_inc(turned, 1)
                pe.wait_ge(taken, i + 1)

        @block.vector
        def _(dve):
            v = nc.vector
            with dve.Fori(0, NT) as i:
                count = 0

                def step(last):
                    nonlocal count
                    count += 1
                    last.then_inc(steps, 1)
                    wait_alone(dve, steps, i * STEPS + count)

                def best(values, out, index, first):
                    for x, o in zip(values, out):
                        last = v.max(o[:, first:first + 8], x)
                    step(last)
                    for x, o, n in zip(values, out, index):
                        last = v.max_index(n[:, first:first + 8], o[:, first:first + 8], x)
                    if first == 0:
                        step(last)
                        for x, o in zip(values, out):
                            last = v.match_replace(x, o[:, 0:8], x, -3.0e38)
                    step(last)

                wait_alone(dve, copied, i + 1)
                halves = [(h, k) for h in range(HEADS) for k in range(2)]
                for first in (0, 8):
                    best([s[:, 2 * h + k, :] for h, k in halves], [val[:, h, k, :] for h, k in halves],
                         [idx[:, h, k, :] for h, k in halves], first)
                grid = [P, HEADS, TOPK, TOPK]
                along = lambda ap: ap.rearrange("p h (a b) -> p h a b", b=1).broadcast_to(grid)
                across = lambda ap: ap.rearrange("p h (a b) -> p h a b", a=1).broadcast_to(grid)
                square = lambda ap: ap.rearrange("p h (a b) -> p h a b", b=TOPK)
                v.tensor_copy(idxf[:, :, :, :], idx[:, :, :, :])
                step(v.tensor_tensor(square(cand[:, :, :]), along(val[:, :, 0, :]), across(val[:, :, 1, :]), ALU.add))
                for first in (0, 8):
                    best([cand[:, h, :] for h in range(HEADS)], [top[:, h, :] for h in range(HEADS)],
                         [pos[:, h, :] for h in range(HEADS)], first)
                v.tensor_scalar(rank[:, 0, :, :], pos[:, :, :], 4, None, ALU.logical_shift_right)
                v.tensor_scalar(rank[:, 1, :, :], pos[:, :, :], 15, None, ALU.bitwise_and)
                gate = picked[:, 2, :].rearrange("p (h k) -> p h k", k=TOPK)
                v.tensor_tensor(gate, top[:, :, :], top[:, :, 0:1].broadcast_to([P, HEADS, TOPK]),
                                ALU.subtract).then_inc(shifted, 1)
                dve.wait_ge(shifted, i + 1)
                v.tensor_copy(rankf[:, :, :, :], rank[:, :, :, :]).then_inc(ranks_done, 1)
                dve.wait_ge(ranks_done, i * 4 + 1)
                ranks = c["iotaf"][:, :].rearrange("p (h a b) -> p h a b", h=1, a=1).broadcast_to(grid)
                for k in range(2):
                    last = v.tensor_tensor(square(match[:, k, :, :]), ranks, along(rankf[:, k, :, :]), ALU.is_equal)
                last.then_inc(ranks_done, 1)
                dve.wait_ge(ranks_done, i * 4 + 2)
                for k in range(2):
                    last = v.tensor_tensor(square(match[:, k, :, :]), square(match[:, k, :, :]),
                                           across(idxf[:, :, k, :]), ALU.mult)
                last.then_inc(ranks_done, 1)
                dve.wait_ge(ranks_done, i * 4 + 3)
                for k in range(2):
                    v.tensor_reduce(picked[:, k, :].rearrange("p (h k) -> p h k", k=TOPK), square(match[:, k, :, :]),
                                    AX_X, ALU.add)
                dve.wait_ge(exped, i + 1)
                step(v.tensor_reduce(total[:, :], gate, AX_X, ALU.add))
                step(v.reciprocal(total[:, :], total[:, :]))
                v.tensor_tensor(gate, gate, total[:, :].rearrange("p (h a) -> p h a", a=1).broadcast_to([P, HEADS, TOPK]),
                                ALU.mult).then_inc(picked_done, 1)
                assert count == STEPS, count
                dve.wait_ge(turned, i + 1)
                at = lambda k: routed[:, k, bass.ds(i * P, P)]
                v.tensor_copy(at(0), ps[:, 0:P])
                v.tensor_copy(at(1), ps[:, P:2 * P])
                v.tensor_scalar(part16[:, :], ps[:, 2 * P:3 * P], 4096.0, None, ALU.mult)
                v.tensor_scalar(whole[:, :], ps[:, 2 * P:3 * P], 4096.0, None, ALU.mult).then_inc(ranks_done, 1)
                dve.wait_ge(ranks_done, i * 4 + 4)
                v.tensor_copy(at(2), part16[:, :])
                v.tensor_tensor(at(3), whole[:, :], part16[:, :], ALU.subtract).then_inc(taken, 1)
                dve.wait_ge(taken, i + 1)


def gate_matrix(nc, c, dram):
    GROUP = 4
    SLOTS = 4
    TURNS = P // (GROUP * SLOTS)
    with ExitStack() as own:
        sb = lambda name, shape, dt=F32: c["sb"](own, name, shape, dt)
        sem = lambda name: own.enter_context(nc.semaphore(name))
        first, second, high, low = (sb(name, [P, SLOTS, GROUP, KEYS], F16)
                                    for name in ("first_hot", "second_hot", "second_hi", "second_lo"))
        out = [sb(f"gate_rows{b}", [P, KEYS, P]) for b in range(2)]
        ps = own.enter_context(nc.psum_tensor("psG", [P, SLOTS, 512], F32))
        hot, high_ready, low_ready = sem("one_hot_ready"), sem("high_ready"), sem("low_ready")
        used, moved = sem("one_hot_used"), sem("gates_moved")
        stored = [sem(f"gates_stored{b}") for b in range(2)]
        block = own.enter_context(nc.Block())
        routed = c["routed"]

        @block.vector
        def _(dve):
            def group(i, b, fresh):
                g = i * SLOTS + b
                if not fresh:
                    dve.wait_ge(used, g - (SLOTS - 1))
                for q in range(GROUP):
                    col = lambda k: routed[:, k, bass.ds(g * GROUP + q, 1)]
                    nc.vector.tensor_scalar(first[:, b, q, :], c["iota"][:, :], col(0), None, ALU.is_equal)
                    last = nc.vector.tensor_scalar(second[:, b, q, :], c["iota"][:, :], col(1), None, ALU.is_equal)
                last.then_inc(hot, 1)

            for b in range(SLOTS):
                group(0, b, True)
            with dve.Fori(1, NT * TURNS) as i:
                for b in range(SLOTS):
                    group(i, b, False)

        @block.gpsimd
        def _(pool):
            with pool.Fori(0, NT * TURNS) as i:
                for b in range(SLOTS):
                    wait_alone(pool, hot, i * SLOTS + (b + 1))
                    part = routed[:, 3, bass.ds(i * SLOTS * GROUP + b * GROUP, GROUP)].rearrange(
                        "p (t a) -> p t a", a=1).broadcast_to([P, GROUP, KEYS])
                    nc.gpsimd.tensor_tensor(low[:, b, :, :], second[:, b, :, :], part, ALU.mult).then_inc(low_ready, 1)

        @block.tensor
        def _(pe):
            def group(i, b, fresh):
                pe.wait_ge(high_ready, i * SLOTS + (b + 1))
                pe.wait_ge(low_ready, i * SLOTS + (b + 1))
                if not fresh:
                    pe.wait_ge(moved, i * SLOTS + (b + 1 - SLOTS))
                for q in range(GROUP):
                    o = ps[:, b, q * KEYS:(q + 1) * KEYS]
                    nc.tensor.matmul(o, first[:, b, q, :], high[:, b, q, :], start=True, stop=False)
                    last = nc.tensor.matmul(o, first[:, b, q, :], low[:, b, q, :], start=False, stop=True)
                last.then_inc(used, 1)

            for b in range(SLOTS):
                group(0, b, True)
            with pe.Fori(1, NT * TURNS) as i:
                for b in range(SLOTS):
                    group(i, b, False)

        @block.scalar
        def _(act):
            def raise_high(i, b, at):
                act.wait_ge(hot, i * SLOTS + (at + b + 1))
                for q in range(GROUP):
                    col = routed[:, 2, bass.ds(i * SLOTS * GROUP + ((at + b) * GROUP + q), 1)]
                    last = nc.scalar.activation(high[:, b % SLOTS, q, :], second[:, b % SLOTS, q, :], ACT.Copy, scale=col)
                last.then_inc(high_ready, 1)

            def turn(tile, i, last):
                at = tile * TURNS * SLOTS
                for b in range(SLOTS):
                    if not (last and b == SLOTS - 1):
                        raise_high(i, b + 1, at)
                    act.wait_ge(used, i * SLOTS + (at + b + 1))
                    rows = out[tile % 2][:, :, bass.ds(i * SLOTS * GROUP + b * GROUP, GROUP)].rearrange("p j t -> p t j")
                    nc.scalar.activation(rows, ps[:, b, :].rearrange("p (t j) -> p t j", j=KEYS), ACT.Copy,
                                         scale=1.0 / 4096).then_inc(moved, 1)

            raise_high(0, 0, 0)
            for tile in range(NT):
                if tile >= 2:
                    act.wait_ge(stored[tile % 2], 16 * (tile // 2))
                final = tile == NT - 1
                with act.Fori(0, TURNS - final) as i:
                    turn(tile, i, False)
                if final:
                    turn(tile, TURNS - 1, True)

        @block.sync
        def _(sp):
            for tile in range(NT):
                sp.wait_ge(moved, (tile + 1) * TURNS * SLOTS)
                sp.dma_start(dram[:, :, tile * P:(tile + 1) * P].rearrange("j i t -> i j t"),
                             out[tile % 2][:, :, :]).then_inc(stored[tile % 2], 16)
            for b in range(2):
                sp.wait_ge(stored[b], 32)


def experts(nc, c, gates_dram, u_dram, v_dram, out):
    R = 4
    TURNS = KEYS // R
    with ExitStack() as own:
        sb = lambda name, shape, dt=F32: c["sb"](own, name, shape, dt)
        sem = lambda name: own.enter_context(nc.semaphore(name))
        u, vt = sb("u_raw", [P, R, DC, P]), sb("v_raw", [P, R, D])
        uh, ul = sb("u_hi", [P, R, DC, P], F32R), sb("u_lo", [P, R, DC, P], F32R)
        vh, vl = sb("v_hi", [P, R, D], F32R), sb("v_lo", [P, R, D], F32R)
        gate = sb("gate_in", [P, R, SEQ])
        acts = sb("gelu", [P, 2, SEQ])
        wh, wl = sb("w_hi", [P, R, SEQ], F32R), sb("w_lo", [P, R, SEQ], F32R)
        h, xh, xl = c["h"], c["x2h"], c["x2l"]
        ps = own.enter_context(nc.psum_tensor("psE", [P, 8, 512], F32))
        u_in, v_in, g_in = ([sem(f"{n}_in{s}") for s in range(R)] for n in "uvg")
        names = "u_hi u_lo v_hi v_lo u_used gelu_done weighted w_hi w_lo y_ready y_added out_stored".split()
        S = {n: sem("e_" + n) for n in names}
        block = own.enter_context(nc.Block())

        def turns(eng, turn):
            turn(0, True, False)
            with eng.Fori(1, TURNS - 1) as i:
                turn(i, False, False)
            turn(TURNS - 1, False, True)

        @block.sync
        def _(sp):
            def at(dram, j, pattern):
                return dram[j] if isinstance(j, int) else dram[bass.ds(j, 1)].rearrange(pattern)

            def load_u(j, r):
                sp.dma_start(u[:, r, :, :], at(u_dram, j, "a p c i -> (a p) c i")).then_inc(u_in[r], 16)

            def load_v(j, r):
                sp.dma_start(vt[:, r, :], at(v_dram, j, "a i d -> (a i) d")).then_inc(v_in[r], 16)

            def load_gates(j, r):
                sp.dma_start(gate[:, r, :], at(gates_dram, j, "a i t -> (a i) t")).then_inc(g_in[r], 16)

            def reload(load, freed, i, slots):
                for r in slots:
                    sp.wait_ge(S[freed], i * R + (r - R + 1))
                    load(i * R + r, r)

            def turn(i, last):
                reload(load_u, "u_lo", i, (2, 3))
                reload(load_v, "v_lo", i, (0, 1))
                reload(load_gates, "weighted", i, (0, 1))
                if not last:
                    reload(load_u, "u_lo", i + 1, (0, 1))
                reload(load_v, "v_lo", i, (2, 3))
                reload(load_gates, "weighted", i, (2, 3))

            for load in (load_u, load_v, load_gates):
                for r in range(R):
                    load(r, r)
            reload(load_u, "u_lo", 1, (0, 1))
            with sp.Fori(1, TURNS - 1) as i:
                turn(i, False)
            turn(TURNS - 1, True)
            for k in range(DC):
                sp.wait_ge(S["y_added"], 16 * TURNS - DC + k + 1)
                sp.dma_start(out[k], h[:, k, :]).then_inc(S["out_stored"], 16)
            sp.wait_ge(S["out_stored"], 16 * DC)

        @block.scalar
        def _(act):
            def split_u(i, r, first):
                act.wait_ge(u_in[r], i * 16 + 16)
                if not first:
                    act.wait_ge(S["u_used"], i * R + (r - R + 1))
                nc.scalar.activation(uh[:, r, :, :], u[:, r, :, :], ACT.Copy).then_inc(S["u_hi"], 1)

            def split_v(i, r, first):
                act.wait_ge(v_in[r], i * 16 + 16)
                if not first:
                    act.wait_ge(S["y_ready"], i * 16 - (8 if r < 2 else 0))
                nc.scalar.activation(vh[:, r, :], vt[:, r, :], ACT.Copy).then_inc(S["v_hi"], 1)

            def gelu(i, r, first):
                act.wait_ge(S["u_used"], i * R + (r + 1))
                if not (first and r < 2):
                    act.wait_ge(S["w_lo"], i * R + (r - 1))
                nc.scalar.activation(acts[:, r % 2, :], ps[:, r % 2, :], ACT.Gelu).then_inc(S["gelu_done"], 1)

            def split_w(i, r):
                act.wait_ge(S["weighted"], i * R + (r + 1))
                nc.scalar.activation(wh[:, r, :], acts[:, r % 2, :], ACT.Copy).then_inc(S["w_hi"], 1)

            def turn(i, first, last):
                for group in (0, 2):
                    for r in (group, group + 1):
                        if group == 0:
                            split_u(i, r + 2, first)
                        elif not last:
                            split_u(i + 1, r - 2, False)
                    for r in (group, group + 1):
                        split_v(i, r, first)
                    for r in (group, group + 1):
                        gelu(i, r, first)
                        split_w(i, r)

            split_u(0, 0, True)
            split_u(0, 1, True)
            turns(act, turn)

        @block.vector
        def _(dve):
            v = nc.vector

            def low_u(i, r):
                dve.wait_ge(S["u_hi"], i * R + (r + 1))
                v.tensor_tensor(ul[:, r, :, :], u[:, r, :, :], uh[:, r, :, :].bitcast(F32),
                                ALU.subtract).then_inc(S["u_lo"], 1)

            def low_v(i, r):
                dve.wait_ge(S["v_hi"], i * R + (r + 1))
                v.tensor_tensor(vl[:, r, :], vt[:, r, :], vh[:, r, :].bitcast(F32), ALU.subtract).then_inc(S["v_lo"], 1)

            def weigh(i, r):
                dve.wait_ge(S["gelu_done"], i * R + (r + 1))
                dve.wait_ge(g_in[r], i * 16 + 16)
                v.tensor_tensor(acts[:, r % 2, :], acts[:, r % 2, :], gate[:, r, :], ALU.mult).then_inc(S["weighted"], 1)

            def low_w(i, r):
                dve.wait_ge(S["w_hi"], i * R + (r + 1))
                v.tensor_tensor(wl[:, r, :], acts[:, r % 2, :], wh[:, r, :].bitcast(F32),
                                ALU.subtract).then_inc(S["w_lo"], 1)

            def add(n, at, m, first=False):
                dve.wait_ge(S["y_ready"], n + (at + m + 1))
                if not first:
                    dve.wait_ge(S["y_added"], n + (at + m + 1 - DC))
                v.tensor_tensor(h[:, m, :], h[:, m, :], ps[:, 4 + m % 4, :], ALU.add).then_inc(S["y_added"], 1)

            def turn(i, first, last):
                for group in (0, 2):
                    for r in (group, group + 1):
                        if group == 0:
                            low_u(i, r + 2)
                        elif not last:
                            low_u(i + 1, r - 2)
                    for r in (group, group + 1):
                        low_v(i, r)
                    adds = [] if first and group == 0 else list(range(DC))
                    at, start = (-8, False) if group == 0 else (0, first)
                    weigh(i, group)
                    low_w(i, group)
                    for m in adds[:2]:
                        add(i * 16, at, m, start)
                    weigh(i, group + 1)
                    for m in adds[2:4]:
                        add(i * 16, at, m, start)
                    low_w(i, group + 1)
                    for m in adds[4:]:
                        add(i * 16, at, m, start)

            low_u(0, 0)
            low_u(0, 1)
            turns(dve, turn)
            for m in range(DC):
                add(TURNS * 16, -8, m)

        @block.tensor
        def _(pe):
            def activations(i, r, first):
                pe.wait_ge(S["u_lo"], i * R + (r + 1))
                if not (first and r < 2):
                    pe.wait_ge(S["gelu_done"], i * R + (r - 1))
                for k in range(DC):
                    last = products(nc, ps[:, r % 2, :], (uh[:, r, k, :], ul[:, r, k, :]),
                                    (xh[:, k, :], xl[:, k, :]), k == 0, k == DC - 1)
                last.then_inc(S["u_used"], 1)

            def outputs(n, at, r0, w_done, first=False):
                pe.wait_ge(S["w_lo"], w_done)
                pe.wait_ge(S["v_lo"], w_done)
                for m in range(DC):
                    if not (first and m < 4):
                        pe.wait_ge(S["y_added"], n + (at + m - 3))
                    for r in (r0, r0 + 1):
                        cols = slice(m * P, (m + 1) * P)
                        last = products(nc, ps[:, 4 + m % 4, :], (vh[:, r, cols], vl[:, r, cols]),
                                        (wh[:, r, :], wl[:, r, :]), r == r0, r == r0 + 1)
                    last.then_inc(S["y_ready"], 1)

            def turn(i, first, last):
                activations(i, 0, first)
                activations(i, 1, first)
                if not first:
                    outputs(i * 16, -8, 2, i * R)
                activations(i, 2, first)
                activations(i, 3, first)
                outputs(i * 16, 0, 0, i * R + 2, first)

            turns(pe, turn)
            outputs(TURNS * 16, -8, 2, TURNS * R)


def build(nc, ap, out):
    gates = nc.dram_tensor("mix_gates", (2 * DC, P, SEQ), F32).ap()
    gate_rows = nc.dram_tensor("expert_gates", (KEYS, KEYS, SEQ), F32).ap()
    with ExitStack() as ctx:
        c = {"sb": lambda own, name, shape, dt=F32: own.enter_context(nc.sbuf_tensor(name, shape, dt))}
        c["dma_sem"] = lambda name: ctx.enter_context(nc.semaphore(name))
        build_constants(nc, ctx, c)
        persistent(nc, ctx, c)
        load_small(nc, c, ap)
        with ExitStack() as mixing:
            c["mixed"] = c["sb"](mixing, "mixed", [P, DC, SEQ])
            with ExitStack() as mixers:
                mixer_buffers(nc, mixers, c)
                input_projections(nc, c, ap["xT"], ap["w_v"], ap["w_full"], ap["w_xonly"], ap["w_ba"], ap["gain1"],
                                  gates)
                token_scalars(nc, c)
                head_pairs(nc, c)
                clear_semaphores(nc)
            mix_and_add(nc, c, ap["w_mixers"], ap["w_o"], gates, ap["xT"])
        c["x2h"], c["x2l"] = (c["sb"](ctx, name, [P, DC, SEQ], F32R) for name in ("x2h", "x2l"))
        c["routed"] = c["sb"](ctx, "routed", [P, 4, SEQ], F32)
        with ExitStack() as routing:
            c["scores"] = c["sb"](routing, "scores", [P, NT, 2 * HEADS, KEYS])
            peer_scores(nc, c, ap["w_q"], ap["keys"])
            route(nc, c)
        gate_matrix(nc, c, gate_rows)
        experts(nc, c, gate_rows, ap["peer_u"], ap["peer_v"], out)


def clear_semaphores(nc):
    numbers = sorted(nc.released_uncleared_semaphores)
    with nc.Block() as block:

        @block.gpsimd
        def _(pool):
            first = 0
            for k, number in enumerate(numbers):
                if k + 1 == len(numbers) or numbers[k + 1] != number + 1:
                    pool.sem_clear(range(numbers[first], number + 1))
                    first = k + 1


def persistent(nc, ctx, c):
    sb = c["sb"]
    c["gains"] = sb(ctx, "gains", [P, DC])
    c["small"] = sb(ctx, "small", [P, 28])
    c["conv_w"] = sb(ctx, "conv_w", [P, 3, PAIRS, 4])
    c["h"] = sb(ctx, "h", [P, DC, SEQ])


def mixer_buffers(nc, ctx, c):
    sb = c["sb"]
    c["proj"] = sb(ctx, "proj", [P, 16, TOK])
    c["qz"] = sb(ctx, "qz", [P, 8, SEQ])
    c["v"] = sb(ctx, "v", [P, NT + 1, SEQ])
    c["ba"] = sb(ctx, "ba", [P, NT + 1, 16])
    c["scalars"] = sb(ctx, "scalars", [P, 6, NT + 1, HEADS])


def load_small(nc, c, ap):
    with ExitStack() as own:
        loaded = own.enter_context(nc.semaphore("smalls_loaded"))
        scaled = own.enter_context(nc.semaphore("gain_scaled"))
        block = own.enter_context(nc.Block())

        @block.sync
        def _(sp):
            sp.dma_start(c["small"][:, :], ap["small"]).then_inc(loaded, 16)
            sp.dma_start(c["conv_w"][:, :, :, :], ap["conv_w"]).then_inc(loaded, 16)
            sp.wait_ge(loaded, 32)

        @block.vector
        def _(dve):
            dve.wait_ge(loaded, 32)
            nc.vector.tensor_scalar(c["small"][:, 16:17], c["small"][:, 16:17], HD ** -0.5, None,
                                    ALU.mult).then_inc(scaled, 1)
            dve.wait_ge(scaled, 1)


def layouts(inputs):
    import numpy as np

    w = {k: np.asarray(v) for k, v in inputs.items()}
    x = np.concatenate([w["meta_tokens"], w["x"][0]], axis=0)

    def chunks(m):
        rows, cols = m.shape
        return np.ascontiguousarray(m.reshape(rows // P, P, cols // P, P).transpose(2, 1, 0, 3))

    w_in = w["w_in"][0]
    cuts = np.cumsum([512, 512, 512, 1536, 512, 8, 8, 1024])
    q, k, v, qkv, z, b, a, gsb, gdn = np.split(w_in, cuts, axis=1)
    ba = np.concatenate([b, a], axis=1).reshape(DC, P, 16).transpose(1, 0, 2)
    col = lambda g: np.concatenate([g, g]).reshape(P, 1)
    row = lambda g: np.broadcast_to(g.reshape(1, -1), (P, g.size))
    small = np.concatenate([row(w["dn_a_log"][0]), row(w["dn_dt_bias"][0]), col(w["sb_q_norm_g"][0]),
                            col(w["sb_k_norm_g"][0]), col(w["dn_out_norm_g"][0]), w["norm2_g"][0].reshape(DC, P).T,
                            np.zeros((P, 1), np.float32)], axis=1)
    mixers = np.concatenate([w["w_sb_out"][0], w["w_dn_out"][0]], axis=0)
    u = w["peer_u"][0].reshape(KEYS, KEYS, DC, P).transpose(1, 3, 2, 0)
    vt = w["peer_v"][0].reshape(KEYS, KEYS, D).transpose(1, 0, 2)
    out = {
        "xT": x.T.reshape(DC, P, TOK), "w_v": chunks(v), "w_full": chunks(np.concatenate([k, qkv], axis=1)),
        "w_xonly": chunks(np.concatenate([q, z, gsb, gdn], axis=1)), "w_ba": ba,
        "gain1": w["norm1_g"][0].reshape(DC, P).T, "small": small,
        "conv_w": w["dn_conv_w"][0].reshape(4, 3, PAIRS, P).transpose(3, 1, 2, 0),
        "w_mixers": chunks(mixers), "w_o": chunks(w["w_o"][0]), "w_q": chunks(w["peer_w_q"][0]),
        "keys": w["peer_sub_keys"][0].transpose(2, 0, 1), "peer_u": u, "peer_v": vt,
    }
    return {name: np.ascontiguousarray(value) for name, value in out.items()}


def kernel(**inputs):
    import numpy as np
    import concourse.bacc as bacc
    from concourse.bass_utils import run_bass_kernel_spmd

    nc = bacc.Bacc("TRN2", target_bir_lowering=False, num_devices=1)
    arrays = {f"in_{name}": a for name, a in layouts(inputs).items()}
    ap = {name[3:]: nc.dram_tensor(name, a.shape, F32, kind="ExternalInput").ap() for name, a in arrays.items()}
    out = nc.dram_tensor("out", (DC, P, SEQ), F32, kind="ExternalOutput").ap()
    build(nc, ap, out)
    r = run_bass_kernel_spmd(nc, [arrays], core_ids=[0])
    y = np.asarray(r.results[0]["out"]).reshape(D, SEQ)
    return np.ascontiguousarray(y.T).reshape(1, SEQ, D)
```
